# Optimizing a Trainium2 kernel written in Bass

```python
import jax, jax.numpy as jnp
from jax import lax
import numpy as np
import math
import jax
import jax.numpy as jnp

D_MODEL = 1024
BATCH = 1
SEQ = 256
DEPTH = 2

HEAD_DIM = 64
N_SB = 6
N_DSA = 6
N_IDX = 8
IDX_DIM = 64
TOPK_MAX = 256
N_HG = 4
HG_DK = 128
HG_DV = 64
D_FF = 4 * D_MODEL
ROPE_THETA = 500000.0
ROT_DIM = HEAD_DIM // 4
Q_BLOCK = 128
HG_CHUNK = 64
EPS = 1e-6
F_MIN = 1e-12
NEG = -1e30
W_SB = N_SB * HEAD_DIM
W_DSA = N_DSA * HEAD_DIM
W_HF = N_HG * HG_DK
W_HV = N_HG * HG_DV
IDX_SCALE = (IDX_DIM * N_IDX) ** -0.5
SPLITS = (W_SB, W_SB, W_SB,
          W_DSA, HEAD_DIM, HEAD_DIM,
          N_IDX * IDX_DIM, IDX_DIM, N_IDX,
          W_HF, W_HF, W_HV, W_HV,
          D_MODEL, D_MODEL, D_MODEL)
D_IN = sum(SPLITS)


def _split_points():
    return [int(v) for v in np.cumsum(np.array(SPLITS))[:-1]]

def rms_norm(x, gain):
    xf = x.astype(jnp.float32)
    y = xf * lax.rsqrt(jnp.mean(xf * xf, axis=-1, keepdims=True) + EPS)
    return (y * gain.astype(jnp.float32)).astype(x.dtype)

def partial_rope(x, pos):
    half = ROT_DIM // 2
    inv = ROPE_THETA ** (-(jnp.arange(half, dtype=jnp.float32) * 2.0) / ROT_DIM)
    ang = pos.astype(jnp.float32)[:, None] * inv[None, :]
    cos = jnp.cos(ang)[None, :, None, :]
    sin = jnp.sin(ang)[None, :, None, :]
    xr = x[..., :ROT_DIM].astype(jnp.float32)
    x1, x2 = xr[..., :half], xr[..., half:]
    rot = jnp.concatenate([x1 * cos - x2 * sin, x2 * cos + x1 * sin], axis=-1).astype(x.dtype)
    return jnp.concatenate([rot, x[..., ROT_DIM:]], axis=-1)

def stick_breaking_attention(q, k, v):
    B, T, H, D = q.shape
    scale = D ** -0.5
    outs = []
    for blk in range(T // Q_BLOCK):
        q0, q1 = blk * Q_BLOCK, (blk + 1) * Q_BLOCK
        z = jnp.einsum('bqhd,bkhd->bhqk', q[:, q0:q1], k[:, :q1]).astype(jnp.float32) * scale
        t_pos = q0 + jnp.arange(Q_BLOCK)[:, None]
        s_pos = jnp.arange(q1)[None, :]
        past = s_pos < t_pos
        log_1m = jnp.where(past, jax.nn.log_sigmoid(-z), 0.0)
        later = lax.cumsum(log_1m, axis=3, reverse=True) - log_1m
        log_a = jnp.where(past, jax.nn.log_sigmoid(z) + later, NEG)
        a = jnp.exp(log_a)
        outs.append(jnp.einsum('bhqk,bkhd->bqhd', a.astype(v.dtype), v[:, :q1]))
    return jnp.concatenate(outs, axis=1)

def dsa_attention(q, k, v, q_idx, k_idx, w_idx):
    B, T, H, D = q.shape
    k_top = min(TOPK_MAX, T // 4)
    gather = jax.vmap(lambda arr, idx: arr[idx])
    outs = []
    for blk in range(T // Q_BLOCK):
        q0, q1 = blk * Q_BLOCK, (blk + 1) * Q_BLOCK
        kl = min(T, max(q1, k_top))
        rel = jax.nn.relu(jnp.einsum('bqjd,bkd->bqjk', q_idx[:, q0:q1], k_idx[:, :kl]).astype(jnp.float32))
        score = jnp.einsum('bqj,bqjk->bqk', w_idx[:, q0:q1].astype(jnp.float32) * IDX_SCALE, rel)
        t_pos = q0 + jnp.arange(Q_BLOCK)[:, None]
        s_pos = jnp.arange(kl)[None, :]
        score = jnp.where(s_pos <= t_pos, score, NEG)
        top_score, top_idx = lax.top_k(score, k_top)
        k_sel = gather(k, top_idx)
        v_sel = gather(v, top_idx)
        logits = jnp.einsum('bqhd,bqkd->bhqk', q[:, q0:q1], k_sel).astype(jnp.float32) * (D ** -0.5)
        valid = (top_score > 0.5 * NEG)[:, None]
        logits = jnp.where(valid, logits, NEG)
        p = jax.nn.softmax(logits, axis=-1)
        outs.append(jnp.einsum('bhqk,bqkd->bqhd', p.astype(v.dtype), v_sel))
    return jnp.concatenate(outs, axis=1)

def hgrn2(q, f_pre, inp, lb):
    B, T, H, DK = q.shape
    DV = inp.shape[-1]
    C = HG_CHUNK
    N = T // C
    q = jax.nn.silu(q.astype(jnp.float32))
    lb = lb.astype(jnp.float32)
    f = lb + (1.0 - lb) * jax.nn.sigmoid(f_pre.astype(jnp.float32))
    log_f = jnp.log(jnp.maximum(f, F_MIN))
    k = 1.0 - f

    def to_chunks(a):
        return a.reshape(B, N, C, H, a.shape[-1]).transpose(1, 0, 3, 2, 4)

    qc, kc, vc, gc = (to_chunks(a) for a in (q, k, inp.astype(jnp.float32), log_f))
    causal = jnp.tril(jnp.ones((C, C), dtype=bool))[:, :, None]

    def step(S, xs):
        qt, kt, vt, gt = xs
        b = jnp.cumsum(gt, axis=2)
        diff = b[:, :, :, None, :] - b[:, :, None, :, :]
        decay = jnp.exp(jnp.where(causal, diff, NEG))
        att = jnp.einsum('bhtk,bhsk,bhtsk->bhts', qt, kt, decay)
        o = jnp.einsum('bhts,bhsv->bhtv', att, vt) + jnp.einsum('bhtk,bhkv->bhtv', qt * jnp.exp(b), S)
        b_last = b[:, :, -1:, :]
        S = S * jnp.exp(b_last[:, :, 0, :, None]) + jnp.einsum('bhsk,bhsv->bhkv', kt * jnp.exp(b_last - b), vt)
        return S, o

    S0 = jnp.zeros((B, H, DK, DV), jnp.float32)
    _, o = lax.scan(step, S0, (qc, kc, vc, gc))
    return o.transpose(1, 0, 3, 2, 4).reshape(B, T, H, DV).astype(inp.dtype)

def hybrid_mixer(h, w_in_l, qn, kn, lb, onorm, w_sb_l, w_dsa_l, w_hg_l, w_out_l):
    B, T, _ = h.shape
    pos = jnp.arange(T)
    (sq, sk, sv, dq, dk, dv, iq, ik, iw, hq, hf, hi, hg,
     g_sb, g_dsa, g_hg) = jnp.split(h @ w_in_l, _split_points(), axis=-1)
    heads = lambda a, n: a.reshape(B, T, n, -1)
    y_sb = stick_breaking_attention(heads(sq, N_SB), heads(sk, N_SB), heads(sv, N_SB)).reshape(B, T, W_SB) @ w_sb_l
    q = partial_rope(rms_norm(heads(dq, N_DSA), qn), pos)
    k = partial_rope(rms_norm(dk[:, :, None, :], kn), pos)[:, :, 0]
    q_i = partial_rope(heads(iq, N_IDX), pos)
    k_i = partial_rope(ik[:, :, None, :], pos)[:, :, 0]
    y_dsa = dsa_attention(q, k, dv, q_i, k_i, iw).reshape(B, T, W_DSA) @ w_dsa_l
    o = hgrn2(heads(hq, N_HG), heads(hf, N_HG), heads(hi, N_HG), lb.reshape(N_HG, HG_DK))
    o = rms_norm(o, onorm) * jax.nn.silu(heads(hg, N_HG))
    y_hg = o.reshape(B, T, W_HV) @ w_hg_l
    mixed = jax.nn.sigmoid(g_sb) * y_sb + jax.nn.sigmoid(g_dsa) * y_dsa + jax.nn.sigmoid(g_hg) * y_hg
    return mixed @ w_out_l

def first_inputs(seed: int = 0) -> dict:
    key = jax.random.key(seed)
    ks = jax.random.split(key, 16)
    f32 = jnp.float32
    res = (2 * DEPTH) ** -0.5

    def nrm(k, shape, fan_in, g=1.0):
        return jax.random.normal(k, shape, f32) * (g * fan_in ** -0.5)

    def gain(k, shape):
        return 1.0 + 0.02 * jax.random.normal(k, shape, f32)

    return {
        'x': jax.random.normal(ks[0], (BATCH, SEQ, D_MODEL), f32),
        'norm_mix': gain(ks[1], (DEPTH, D_MODEL)),
        'w_in': nrm(ks[2], (DEPTH, D_MODEL, D_IN), D_MODEL),
        'qn_dsa': gain(ks[3], (DEPTH, HEAD_DIM)),
        'kn_dsa': gain(ks[4], (DEPTH, HEAD_DIM)),
        'hgrn_lb': 0.5 * jax.random.normal(ks[5], (DEPTH, W_HF), f32),
        'hgrn_onorm': gain(ks[6], (DEPTH, HG_DV)),
        'w_br_sb': nrm(ks[7], (DEPTH, W_SB, D_MODEL), W_SB),
        'w_br_dsa': nrm(ks[8], (DEPTH, W_DSA, D_MODEL), W_DSA),
        'w_br_hgrn': nrm(ks[9], (DEPTH, W_HV, D_MODEL), W_HV),
        'w_out': nrm(ks[10], (DEPTH, D_MODEL, D_MODEL), D_MODEL, res),
        'norm_mlp': gain(ks[11], (DEPTH, D_MODEL)),
        'w_up': nrm(ks[12], (DEPTH, D_MODEL, D_FF), D_MODEL),
        'w_down': nrm(ks[13], (DEPTH, D_FF, D_MODEL), D_FF, res),
    }

def first_block(x, norm_mix, w_in, qn_dsa, kn_dsa, hgrn_lb, hgrn_onorm, w_br_sb, w_br_dsa,
              w_br_hgrn, w_out, norm_mlp, w_up, w_down):
    p_lb = jax.nn.softmax(hgrn_lb.astype(jnp.float32), axis=0)
    lbs = jnp.cumsum(p_lb, axis=0) - p_lb[0:1]
    for l in range(DEPTH):
        h = rms_norm(x, norm_mix[l])
        x = x + hybrid_mixer(h, w_in[l], qn_dsa[l], kn_dsa[l], lbs[l], hgrn_onorm[l],
                             w_br_sb[l], w_br_dsa[l], w_br_hgrn[l], w_out[l])
        h2 = rms_norm(x, norm_mlp[l])
        x = x + jnp.square(jax.nn.relu(h2 @ w_up[l])) @ w_down[l]
    return x


DEPTH_2 = 1

MEM_LEN = 256
GRID_W = 64
NA_HEADS = D_MODEL // (2 * HEAD_DIM)
NA_WIN_ROWS = 8
NA_WIN_COLS = 16
DIL_PAIRS = ((128, 1), (512, 4), (2048, 16))
DIL_GROUPS = len(DIL_PAIRS)
DIL_HEADS_PER_GROUP = D_MODEL // (4 * HEAD_DIM)
DIL_HEADS = DIL_GROUPS * DIL_HEADS_PER_GROUP
DIL_BLOCK = 128
MEM_HEADS = 4
T5_BUCKETS = 32
T5_MAX_DIST = 1024
N_GROUPS = 4
EXPERTS_PER_GROUP = 8
N_EXPERTS = N_GROUPS * EXPERTS_PER_GROUP
TOP_K = 2
D_EXPERT = D_MODEL // 2
MOE_BLOCK = 256
NEG_INF = -1e30

NA_W = NA_HEADS * HEAD_DIM
DIL_W = DIL_HEADS * HEAD_DIM
DIL_OUT_W = DIL_HEADS_PER_GROUP * HEAD_DIM
MEM_W = MEM_HEADS * HEAD_DIM
IN_COLS = 3 * NA_W + 3 * DIL_W + MEM_W
MIX_W = NA_W + DIL_OUT_W + MEM_W
IN_SPLITS = (NA_W, 2 * NA_W, 3 * NA_W, 3 * NA_W + DIL_W, 3 * NA_W + 2 * DIL_W, 3 * NA_W + 3 * DIL_W)


def rms_norm_2(x, g):
    xf = x.astype(jnp.float32)
    y = xf * lax.rsqrt(jnp.mean(xf * xf, axis=-1, keepdims=True) + EPS)
    return (y * g.astype(jnp.float32)).astype(x.dtype)

def t5_bucket(rel):
    nb = T5_BUCKETS // 2
    max_exact = nb // 2
    n = jnp.abs(rel)
    upper = (rel > 0).astype(jnp.int32) * nb
    nf = jnp.maximum(n, 1).astype(jnp.float32)
    large = max_exact + (jnp.log(nf / max_exact) / math.log(T5_MAX_DIST / max_exact) * (nb - max_exact)).astype(jnp.int32)
    large = jnp.minimum(large, nb - 1)
    return upper + jnp.where(n < max_exact, n, large)

def neighborhood_attention(q, k, v, rpb):
    b, s, h, dh = q.shape
    rows = s // GRID_W
    kh = min(NA_WIN_ROWS, rows)
    kw = NA_WIN_COLS
    kg = k.reshape(b, rows, GRID_W, h, dh).transpose(0, 3, 1, 2, 4)
    vg = v.reshape(b, rows, GRID_W, h, dh).transpose(0, 3, 1, 2, 4)
    qg = q.reshape(b, rows, GRID_W, h, dh).transpose(1, 0, 3, 2, 4)
    cols = jnp.arange(GRID_W)
    c0 = jnp.clip(cols - kw // 2, 0, GRID_W - kw)
    col_idx = c0[:, None] + jnp.arange(kw)[None, :]
    dc = col_idx - cols[:, None] + (NA_WIN_COLS - 1)
    scale = HEAD_DIM ** -0.5

    def row_fn(args):
        q_r, r = args
        r0 = jnp.clip(r - kh // 2, 0, rows - kh)
        k_rows = lax.dynamic_slice_in_dim(kg, r0, kh, axis=2)
        v_rows = lax.dynamic_slice_in_dim(vg, r0, kh, axis=2)
        k_win = k_rows[:, :, :, col_idx]
        v_win = v_rows[:, :, :, col_idx]
        dr = r0 + jnp.arange(kh) - r + (NA_WIN_ROWS - 1)
        bias = rpb[:, dr[:, None, None], dc[None]].transpose(0, 2, 1, 3)
        logits = jnp.einsum('bhcd,bhacjd->bhcaj', q_r, k_win).astype(jnp.float32) * scale + bias.astype(jnp.float32)[None]
        p = jax.nn.softmax(logits, axis=(-2, -1)).astype(v.dtype)
        return jnp.einsum('bhcaj,bhacjd->bhcd', p, v_win)

    out = lax.map(row_fn, (qg, jnp.arange(rows)))
    return out.transpose(1, 0, 3, 2, 4).reshape(b, s, h * dh)

def dilated_window_attention(q, k, v, offs, bias, half):
    b, s, h, dh = q.shape
    scale = HEAD_DIM ** -0.5
    kp = jnp.pad(k, ((0, 0), (half, half), (0, 0), (0, 0)))
    vp = jnp.pad(v, ((0, 0), (half, half), (0, 0), (0, 0)))
    local = jnp.arange(DIL_BLOCK)[:, None] + offs[None, :] + half
    bias32 = bias.astype(jnp.float32)
    n_blk = s // DIL_BLOCK

    def block_fn(i):
        s0 = i * DIL_BLOCK
        qb = lax.dynamic_slice_in_dim(q, s0, DIL_BLOCK, axis=1)
        kb = lax.dynamic_slice_in_dim(kp, s0, DIL_BLOCK + 2 * half, axis=1)
        vb = lax.dynamic_slice_in_dim(vp, s0, DIL_BLOCK + 2 * half, axis=1)
        kgat = kb[:, local]
        vgat = vb[:, local]
        key_pos = s0 + local - half
        valid = (key_pos >= 0) & (key_pos < s)
        logits = jnp.einsum('bqhd,bqjhd->bqhj', qb, kgat).astype(jnp.float32) * scale + bias32[None, None]
        logits = jnp.where(valid[None, :, None, :], logits, NEG_INF)
        m = jnp.max(logits, axis=-1)
        e = jnp.exp(logits - m[..., None])
        den = jnp.sum(e, axis=-1)
        o = jnp.einsum('bqhj,bqjhd->bqhd', e, vgat.astype(jnp.float32)) / den[..., None]
        return o, m, den

    o, m, den = lax.map(block_fn, jnp.arange(n_blk))
    o = o.transpose(1, 0, 2, 3, 4).reshape(b, s, h, dh)
    m = m.transpose(1, 0, 2, 3).reshape(b, s, h)
    den = den.transpose(1, 0, 2, 3).reshape(b, s, h)
    return o, m, den

def hierarchical_moe(h, w_r1, b_r1, w_r2, b_r2, w1, w3, w2):
    b, s, d = h.shape
    n = b * s
    t = h.reshape(n, d)
    grp_logits = (t @ w_r1).astype(jnp.float32) + b_r1.astype(jnp.float32)
    grp_prob = jax.nn.softmax(grp_logits, axis=-1)
    grp_idx = jnp.argmax(grp_logits, axis=-1)
    grp_gate = jnp.take_along_axis(grp_prob, grp_idx[:, None], axis=-1)
    fine_logits = ((t @ w_r2).astype(jnp.float32) + b_r2.astype(jnp.float32)).reshape(n, N_GROUPS, EXPERTS_PER_GROUP)
    fine_sel = jnp.take_along_axis(fine_logits, grp_idx[:, None, None], axis=1)[:, 0]
    top_val, top_idx = lax.top_k(fine_sel, TOP_K)
    gate = grp_gate * jax.nn.softmax(top_val, axis=-1)
    exp_idx = grp_idx[:, None] * EXPERTS_PER_GROUP + top_idx
    n_rows = n * TOP_K
    e_flat = exp_idx.reshape(-1)
    g_flat = gate.reshape(-1)
    tok_flat = jnp.repeat(jnp.arange(n), TOP_K)
    order = jnp.argsort(e_flat)
    e_sorted = e_flat[order]
    counts = jnp.bincount(e_flat, length=N_EXPERTS)
    cnt_start = jnp.cumsum(counts) - counts
    padded = (counts + MOE_BLOCK - 1) // MOE_BLOCK * MOE_BLOCK
    pad_end = jnp.cumsum(padded)
    pad_start = pad_end - padded
    dest = pad_start[e_sorted] + jnp.arange(n_rows) - cnt_start[e_sorted]
    cap = n_rows + N_EXPERTS * MOE_BLOCK
    row_tok = jnp.full((cap,), n, jnp.int32).at[dest].set(tok_flat[order])
    row_gate = jnp.zeros((cap,), jnp.float32).at[dest].set(g_flat[order])
    n_blk = cap // MOE_BLOCK
    blk_exp = jnp.minimum(jnp.searchsorted(pad_end, jnp.arange(n_blk) * MOE_BLOCK, side='right'), N_EXPERTS - 1)
    t_pad = jnp.concatenate([t, jnp.zeros((1, d), t.dtype)], axis=0)
    xs = t_pad[row_tok].reshape(n_blk, MOE_BLOCK, d)

    def expert_block(args):
        xb, e = args
        a = jax.nn.silu(xb @ w1[e]) * (xb @ w3[e])
        return a @ w2[e]

    yb = lax.map(expert_block, (xs, blk_exp)).reshape(cap, d)
    y = jnp.zeros((n + 1, d), h.dtype).at[row_tok].add(yb * row_gate[:, None].astype(h.dtype))
    return y[:n].reshape(b, s, d)

def second_inputs(seed: int = 0) -> dict:
    key = jax.random.key(seed)
    ks = jax.random.split(key, 18)
    f32 = jnp.float32

    def nrm(k, shape, sc):
        return jax.random.normal(k, shape, f32) * sc

    L = DEPTH_2
    return {
        'x': nrm(ks[0], (BATCH, SEQ, D_MODEL), 1.0),
        'mem': nrm(ks[1], (BATCH, MEM_LEN, D_MODEL), 1.0),
        'g_mix': 1.0 + nrm(ks[2], (L, D_MODEL), 0.02),
        'w_in': nrm(ks[3], (L, D_MODEL, IN_COLS), D_MODEL ** -0.5),
        'qk_gain': 1.0 + nrm(ks[4], (L, 3, 2, HEAD_DIM), 0.02),
        'na_rpb': nrm(ks[5], (L, NA_HEADS, 2 * NA_WIN_ROWS - 1, 2 * NA_WIN_COLS - 1), 0.1),
        't5_table': nrm(ks[6], (T5_BUCKETS, DIL_HEADS), 0.1),
        'g_mem': 1.0 + nrm(ks[7], (L, D_MODEL), 0.02),
        'w_mem_kv': nrm(ks[8], (L, D_MODEL, 2 * MEM_W), D_MODEL ** -0.5),
        'w_out': nrm(ks[9], (L, MIX_W, D_MODEL), MIX_W ** -0.5),
        'g_ffn': 1.0 + nrm(ks[10], (L, D_MODEL), 0.02),
        'w_r1': nrm(ks[11], (L, D_MODEL, N_GROUPS), D_MODEL ** -0.5),
        'b_r1': nrm(ks[12], (L, N_GROUPS), 0.01),
        'w_r2': nrm(ks[13], (L, D_MODEL, N_EXPERTS), D_MODEL ** -0.5),
        'b_r2': nrm(ks[14], (L, N_EXPERTS), 0.01),
        'w1': nrm(ks[15], (L, N_EXPERTS, D_MODEL, D_EXPERT), D_MODEL ** -0.5),
        'w3': nrm(ks[16], (L, N_EXPERTS, D_MODEL, D_EXPERT), D_MODEL ** -0.5),
        'w2': nrm(ks[17], (L, N_EXPERTS, D_EXPERT, D_MODEL), D_EXPERT ** -0.5),
    }

def second_block(x, mem, g_mix, w_in, qk_gain, na_rpb, t5_table, g_mem, w_mem_kv, w_out, g_ffn, w_r1, b_r1, w_r2, b_r2, w1, w3, w2):
    b, s, _ = x.shape
    hd = HEAD_DIM
    scale = HEAD_DIM ** -0.5
    t5 = t5_table.reshape(T5_BUCKETS, DIL_GROUPS, DIL_HEADS_PER_GROUP)
    for l in range(DEPTH_2):
        h = rms_norm_2(x, g_mix[l])
        qa, ka, va, qd, kd, vd, qm = jnp.split(h @ w_in[l], IN_SPLITS, axis=-1)

        qa = rms_norm_2(qa.reshape(b, s, NA_HEADS, hd), qk_gain[l, 0, 0])
        ka = rms_norm_2(ka.reshape(b, s, NA_HEADS, hd), qk_gain[l, 0, 1])
        va = va.reshape(b, s, NA_HEADS, hd)
        out_na = neighborhood_attention(qa, ka, va, na_rpb[l])

        dshape = (b, s, DIL_GROUPS, DIL_HEADS_PER_GROUP, hd)
        qd = rms_norm_2(qd.reshape(dshape), qk_gain[l, 1, 0])
        kd = rms_norm_2(kd.reshape(dshape), qk_gain[l, 1, 1])
        vd = vd.reshape(dshape)
        o_list, m_list, d_list = [], [], []
        for g, (win, dil) in enumerate(DIL_PAIRS):
            half = win // 2
            n_side = half // dil
            offs = jnp.arange(-n_side, n_side + 1) * dil
            bias = t5[t5_bucket(offs), g].T
            o, m, den = dilated_window_attention(qd[:, :, g], kd[:, :, g], vd[:, :, g], offs, bias, half)
            o_list.append(o)
            m_list.append(m)
            d_list.append(den)
        m_all = jnp.stack(m_list)
        wts = jnp.stack(d_list) * jnp.exp(m_all - jnp.max(m_all, axis=0, keepdims=True))
        out_dil = jnp.sum(wts[..., None] * jnp.stack(o_list), axis=0) / jnp.sum(wts, axis=0)[..., None]
        out_dil = out_dil.astype(x.dtype).reshape(b, s, DIL_OUT_W)

        kvm = rms_norm_2(mem, g_mem[l]) @ w_mem_kv[l]
        km, vm = jnp.split(kvm, 2, axis=-1)
        km = rms_norm_2(km.reshape(b, -1, MEM_HEADS, hd), qk_gain[l, 2, 1])
        vm = vm.reshape(b, -1, MEM_HEADS, hd)
        qm = rms_norm_2(qm.reshape(b, s, MEM_HEADS, hd), qk_gain[l, 2, 0])
        logits_m = jnp.einsum('bshd,bmhd->bhsm', qm, km).astype(jnp.float32) * scale
        p_m = jax.nn.softmax(logits_m, axis=-1).astype(vm.dtype)
        out_mem = jnp.einsum('bhsm,bmhd->bshd', p_m, vm).reshape(b, s, MEM_W)

        x = x + jnp.concatenate([out_na, out_dil, out_mem], axis=-1) @ w_out[l]
        x = x + hierarchical_moe(rms_norm_2(x, g_ffn[l]), w_r1[l], b_r1[l], w_r2[l], b_r2[l], w1[l], w3[l], w2[l])
    return x


def setup_inputs(seed=0):
    out = dict(first_inputs(seed))
    for name, value in second_inputs(seed + 1).items():
        if name != "x":
            out[name + "_2"] = value
    return out


def reference(
    x, norm_mix, w_in, qn_dsa, kn_dsa, hgrn_lb, hgrn_onorm, w_br_sb, w_br_dsa, w_br_hgrn, w_out,
    norm_mlp, w_up, w_down, mem_2, g_mix_2, w_in_2, qk_gain_2, na_rpb_2, t5_table_2, g_mem_2,
    w_mem_kv_2, w_out_2, g_ffn_2, w_r1_2, b_r1_2, w_r2_2, b_r2_2, w1_2, w3_2, w2_2,
):
    x = first_block(
        x, norm_mix, w_in, qn_dsa, kn_dsa, hgrn_lb, hgrn_onorm, w_br_sb, w_br_dsa, w_br_hgrn,
        w_out, norm_mlp, w_up, w_down,
    )
    return second_block(
        x, mem_2, g_mix_2, w_in_2, qk_gain_2, na_rpb_2, t5_table_2, g_mem_2, w_mem_kv_2,
        w_out_2, g_ffn_2, w_r1_2, b_r1_2, w_r2_2, b_r2_2, w1_2, w3_2, w2_2,
    )


_drawn_inputs = setup_inputs


def setup_inputs(seed=0):
    import zlib

    import numpy as np

    out = dict(_drawn_inputs(seed))
    spreads = {}
    factors = {'norm_mix': 3.234,
     'qn_dsa': 5.829,
     'kn_dsa': 6.961,
     'hgrn_lb': 3.562,
     'hgrn_onorm': 4.469,
     'g_mix_2': 8.0,
     'qk_gain_2': 4.251,
     't5_table_2': 4.041,
     'g_mem_2': 8.0,
     'b_r1_2': 64.0,
     'b_r2_2': 34.768,
     'na_rpb_2': 4.558,
     'g_ffn_2': 8.0}
    for name, (base, spread) in spreads.items():
        noise = np.random.default_rng([zlib.crc32(name.encode()), seed]).standard_normal(out[name].shape)
        drawn = base * np.exp(spread * noise) if base else spread * noise
        out[name] = jnp.asarray(drawn.astype(out[name].dtype))
    for name, factor in factors.items():
        out[name] = (out[name] * factor).astype(out[name].dtype)
    return out
```

```python
import math
from contextlib import ExitStack

import numpy as np

import concourse.bass as bass
from concourse import mybir

F32 = mybir.dt.float32
U32 = mybir.dt.uint32
ALU = mybir.AluOpType
ACT = mybir.ActivationFunctionType
AX = mybir.AxisListType

P = 128
T = 256
NT = T // P
D = 1024
KD = D // P
DEPTH = 2
HD = 64
EPS = 1e-6
F_MIN = 1e-12
NEG = -1e30

N_SB, N_DSA, N_IDX, N_HG, HG_DV, HG_CHUNK = 6, 6, 8, 4, 64, 64
SPLITS = [("sq", 384), ("sk", 384), ("sv", 384), ("dq", 384), ("dk", 64), ("dv", 64), ("iq", 512),
          ("ik", 64), ("iw", 8), ("hq", 512), ("hf", 512), ("hi", 256), ("hg", 256),
          ("gsb", 1024), ("gdsa", 1024), ("ghg", 1024)]
COL = {}
_at = 0
for _n, _w in SPLITS:
    COL[_n] = _at
    _at += _w
D_IN = _at
IDX_SCALE = float((64 * N_IDX) ** -0.5)
TOPK = 64
RH = 18
D_FF = 4 * D
NF = D_FF // P

NA_HEADS, DIL_HPG, DIL_G, MEM_HEADS = 8, 4, 3, 4
IN2 = 4096
GRID = 64
N_EXP, N_GRP, EPG = 32, 4, 8
D_EXP = 512
DIL = ((128, 1), (512, 4), (2048, 16))

SLOTS = 4
MSLOTS = 6
RING = 6


def chunks_of_layer(l):
    c = [("w_in", 0, 8, COL["sq"], 384), ("w_in", 0, 8, COL["sk"], 384), ("w_in", 0, 8, COL["sv"], 384),
         ("w_in", 0, 8, COL["dq"], 512), ("w_in", 0, 8, COL["iq"], 512), ("w_in", 0, 8, COL["ik"], 72),
         ("w_in", 0, 8, COL["hq"], 512), ("w_in", 0, 8, COL["hf"], 512), ("w_in", 0, 8, COL["hi"], 256),
         ("w_in", 0, 8, COL["hg"], 256)]
    c += [("w_in", 0, 8, COL["gsb"] + 512 * j, 512) for j in range(6)]
    c += [("w_br", 0, 8, 512 * j, 512) for j in range(2)]
    c += [("w_out", 0, 8, 512 * j, 512) for j in range(2)]
    c += [("w_up", 0, 8, 512 * j, 512) for j in range(8)]
    c += [("w_down", 1024 * kb, 8, 512 * n, 512) for kb in range(4) for n in range(2)]
    return [(l,) + x for x in c]


def chunks_of_block2():
    c = [("w_mem_kv_2", 0, 8, 0, 512)]
    c += [("w_in_2", 0, 8, 512 * j, 512) for j in range(8)]
    c += [("w_out_2", 0, 8, 512 * j, 512) for j in range(2)]
    return [(0,) + x for x in c]


def mixer_steps():
    s = [("rt", c) for c in range(9)]
    for h in range(N_SB + 2):
        if h < N_SB:
            s.append(("z", h))
        if 1 <= h <= N_SB:
            s.append(("u", h - 1))
        if h >= 3 and h % 2 == 1:
            s.append(("o", (h - 3) // 2))
    s.append(("hp", 0))
    for i in range(NT):
        s += [("ix", i, j) for j in range(N_IDX)]
        s.append(("tk", i))
    s += [("lv", 0), ("lv", 1)]
    for j in range(9):
        if j <= 7:
            s.append(("lm", j))
        s += [("hx",)] if j == 0 else [("hl", j, 0), ("hl", j, 1)]
        if j + 2 <= 7:
            s.append(("lv", j + 2))
    s.append(("ho",))
    n = N_DSA * NT
    for u in range(n + 3):
        for kind, v in (("dl", u), ("dn", u - 1), ("dt", u - 2), ("dp", u - 3)):
            if 0 <= v < n:
                s.append((kind, v))
    s += [("on",), ("oht", 0), ("oht", 1)]
    out, g = [], 0
    for j, x in enumerate(s):
        while g < 24 and g * len(s) <= j * 24:
            out.append(("g", g))
            g += 1
        out.append(x)
    out += [("g", g) for g in range(g, 24)]
    return out


MIX = mixer_steps()


def attn_steps(n):
    s = []
    for u in range(n + 3):
        for kind, v in (("dl", u), ("dn", u - 1), ("dt", u - 2), ("dp", u - 3)):
            if 0 <= v < n:
                s.append((kind, v))
    return s


class Banks:

    def __init__(self, full, free):
        self.full_sem, self.free_sem = full, free
        self.uses = [0] * 8
        self.turn, self.long_turn = 0, 0
        self.at = {}

    def give(self, key, long=False):
        if long:
            b = RING + self.long_turn % 2
            self.long_turn += 1
        else:
            b = self.turn % RING
            self.turn += 1
        assert key not in self.at, key
        self.at[key] = (b, self.uses[b])
        self.uses[b] += 1

    def bank(self, key):
        return self.at[key][0]

    def full(self, key):
        b, u = self.at[key]
        return self.full_sem[b], u + 1

    def freed(self, key):
        b, u = self.at[key]
        return self.free_sem[b], u + 1

    def before(self, key):
        b, u = self.at[key]
        return self.free_sem[b], u


def build(nc, a, out):
    ctx = ExitStack()
    with ctx:
        ctx.enter_context(nc.allow_non_contiguous_dma(reason="parameter columns of a few KiB"))

        def sb(name, shape, dt=F32):
            return ctx.enter_context(nc.sbuf_tensor(name, shape, dt))

        def sem(name):
            return ctx.enter_context(nc.semaphore(name))

        CW = a["c_main"].shape[1]
        ring = sb("ring", [P, SLOTS, KD, 512])
        cst = sb("cst", [P, CW])
        x = sb("x", [P, NT, D])
        hT = sb("hT", [P, KD, T])
        par = sb("par", [P, 1160])
        small = sb("small", [P, 512])
        REGION = 27584
        region = sb("region", [P, REGION])

        class Cutter:

            def __init__(self, tile, end, at=0):
                self.tile, self.end, self.at = tile, end, at

            def cut(self, *dims):
                n = math.prod(dims)
                v = self.tile[:, self.at:self.at + n]
                self.at += n
                assert self.at <= self.end, self.at
                if len(dims) == 2:
                    v = v.rearrange("p (a b) -> p a b", a=dims[0])
                elif len(dims) == 3:
                    v = v.rearrange("p (a b c) -> p a b c", a=dims[0], b=dims[1])
                return v

        c_ = Cutter(cst, CW).cut
        ident, negtri, negones = c_(P), c_(P), c_(P)
        sbmask, sbneg = c_(384), c_(384)
        causal = c_(NT, T)
        hgmask = c_(8, P)
        scan0 = c_(T)
        cosT, sinT = c_(NT, 8), c_(NT, 8)
        nawin = c_(GRID)
        desc = c_(N_EXP)
        p_ = Cutter(par, 1160).cut
        g_mix, g_mlp = p_(DEPTH, KD), p_(DEPTH, KD)
        g_mix2, g_mem2, g_ffn2 = p_(KD), p_(KD), p_(KD)
        lbraw = p_(DEPTH, N_HG)
        qn, kn, onorm = p_(DEPTH, HD), p_(DEPTH, HD), p_(DEPTH, HD)
        qkg = p_(6, HD)
        rbias = p_(36)
        wr = p_(KD, 36)
        s_ = Cutter(small, 512).cut
        eps_c = s_(1)
        ss, sd, rstd = s_(2), s_(2), s_(2)
        lb, omlb = s_(DEPTH, N_HG), s_(DEPTH, N_HG)
        lb_m, lb_s, lb_r = s_(N_HG), s_(N_HG), s_(N_HG)
        lb_e = s_(DEPTH, N_HG)
        ss14, sd14, r14 = s_(NT, 7), s_(NT, 7), s_(NT, 7)
        ss8, sd8, r8 = s_(8), s_(8), s_(8)
        iw = s_(NT, N_IDX)
        top8 = s_(8)
        mx = s_(4, 3)
        nmax, esum, rsum = s_(4), s_(4), s_(4)
        seg_ss, seg_sd, seg_r = s_(NT, 12), s_(NT, 12), s_(NT, 12)

        A = Cutter(region, REGION)
        sqT, skT, sv = A.cut(3, T), A.cut(3, T), A.cut(NT, 384)
        E = [Cutter(region, REGION, 1024 * j).cut(N_HG, T) for j in range(2)]
        dv = A.cut(NT, HD)
        at_RT = A.at
        RT = A.cut(9, T)
        ymul = [Cutter(region, REGION, at_RT + 768 * j).cut(768) for j in range(2)]
        at_R = A.at
        R = A.cut(NT, RH, HD)
        mixT = Cutter(region, REGION, at_R).cut(KD, T)
        hqT = A.cut(N_HG, T)
        at_f = A.at
        fT = A.cut(N_HG, T)
        og, og2 = Cutter(region, REGION, at_f).cut(8, HD), Cutter(region, REGION, at_f + 512).cut(8, HD)
        kT, bT = A.cut(N_HG, T), A.cut(N_HG, T)
        attT, attX = A.cut(N_HG, NT, P), A.cut(N_HG, P)
        hv, hgs = A.cut(NT, T), A.cut(NT, T)
        sbL = [A.cut(384) for _ in range(2)]
        sbA = [A.cut(384) for _ in range(4)]
        at_rel = A.at
        rel = [A.cut(T) for _ in range(2)]
        score, negsel = A.cut(NT, T), A.cut(NT, T)
        osT, odT, ohT = A.cut(3, T), A.cut(3, T), A.cut(2, T)
        prb = [A.cut(T) for _ in range(4)]
        prT = [A.cut(NT, P) for _ in range(3)]
        hsg = [Cutter(region, REGION, at_f + 1024 + 256 * j).cut(T) for j in range(2)]
        gT = A.cut(24, T)
        xn = gT[:, 0:8, :].rearrange("p m t -> p (m t)").rearrange("p (i d) -> p i d", i=NT)
        ra = Cutter(region, REGION, at_rel).cut(896)
        sq14 = ra.rearrange("p (i h d) -> p i h d", i=NT, h=7)
        M = Cutter(region, REGION)
        hid = M.cut(NF, T)
        hrl = [M.cut(T) for _ in range(4)]

        C = Cutter(region, REGION)
        xn2, memT = C.cut(NT, D), C.cut(KD, T)
        PP, kv = C.cut(NT, IN2), C.cut(NT, 512)
        PT = C.cut(24, T)
        na_bias = C.cut(NA_HEADS, 6, GRID)
        dil_bias = C.cut(12, 384)
        xn2_flat = xn2.rearrange("p i d -> p (i d)")
        memT_flat = memT.rearrange("p k t -> p (k t)")
        PT_flat = PT.rearrange("p c t -> p (c t)")
        hT_flat = hT[:, :, :].rearrange("p k t -> p (k t)")
        prb2 = [hT_flat[:, 0:768], hT_flat[:, 768:1536], xn2_flat[:, 0:768], xn2_flat[:, 768:1536]]
        prT2 = [memT_flat[:, 0:768].rearrange("p (s t) -> p s t", s=6),
                memT_flat[:, 768:1536].rearrange("p (s t) -> p s t", s=6),
                PP[:, 0, 2304:3072].rearrange("p (s t) -> p s t", s=6)]
        zero_bias = memT_flat[:, 1536:1792]
        squares = xn2_flat[:, 0:1536]
        t5_onehot, t5_tab = PT_flat[0:32, 0:1536], PT_flat[0:32, 1536:1548]
        t5_mask, t5_rows = PT_flat[0:4, 2048:3584], PT_flat[0:4, 4096:5632]

        def oT2(c):
            return PP[:, c // 4, T * (c % 4):T * (c % 4) + T]

        X = Cutter(region, REGION)
        wslot = [ring[:, j, :, :] for j in range(SLOTS)] + [X.cut(KD, 512) for _ in range(MSLOTS - SLOTS)]
        aT = [X.cut(4, T) for _ in range(2)]
        gate = [X.cut(T) for _ in range(2)]
        sgm = [X.cut(T) for _ in range(2)]
        hm = [X.cut(T) for _ in range(4)]
        xn3 = X.cut(NT, D)
        rl = X.cut(NT, 36)
        grp = [X.cut(NT, N_GRP) for _ in range(6)]
        fine = [X.cut(NT, N_EXP) for _ in range(6)]
        one = [X.cut(NT, 1) for _ in range(12)]
        gateT = X.cut(T)
        zeros = X.cut(P)

        psum = [ctx.enter_context(nc.psum_tensor(f"bank{b}", [P, 512], F32)) for b in range(8)]

        NA_ROW = NA_HEADS * 15 * 31
        na_dram = nc.dram_tensor("na_bias_rows", [GRID, NA_ROW], F32, kind="Internal").ap()
        t5_dram = nc.dram_tensor("t5_bias_rows", [12, P, 512], F32, kind="Internal").ap()
        gate_dram = nc.dram_tensor("gate_rows", [N_EXP, T], F32, kind="Internal").ap()

        bank_full = [sem(f"bank{b}_full") for b in range(8)]
        bank_free = [sem(f"bank{b}_free") for b in range(8)]
        slot_full = [sem(f"slot{j}_full") for j in range(MSLOTS)]
        (down_chunk_used, consts_loaded, x_loaded, params_loaded, eps_set, act_step, dve_step, std_ready,
         rows_normed, log1p_ready, sp_ready, sba_ready, head_sums, head_std, R_ready, sig_ready, f_ready,
         logf_ready, level_exponents, level_exps, level_ready, o_sums, o_std, og_ready, rel_used, rowmax_ready,
         exps_ready, probs_ready, probsT_used, gates_ready, mix_ready, hid_ready, lb_shifted, lb_exps,
         mem_loaded, t5_loaded, t5_masked, t5_stored, bias_loaded, seg_squared, seg_sums, seg_std, seg_normed,
         router_shifted, router_exps, gates_made, gateT_ready, gate_stored, y_step, aT_ready, sig2_ready,
         out_ready, out_stored, na_stored, zeros_set, gain0_loaded) = [sem(n) for n in (
             "down_chunk_used consts_loaded x_loaded params_loaded eps_set act_step dve_step std_ready "
             "rows_normed log1p_ready sp_ready sba_ready head_sums head_std R_ready sig_ready f_ready "
             "logf_ready level_exponents level_exps level_ready o_sums o_std og_ready rel_used rowmax_ready "
             "exps_ready probs_ready probsT_used gates_ready mix_ready hid_ready lb_shifted lb_exps "
             "mem_loaded t5_loaded t5_masked t5_stored bias_loaded seg_squared seg_sums seg_std seg_normed "
             "router_shifted router_exps gates_made gateT_ready gate_stored y_step aT_ready sig2_ready "
             "out_ready out_stored na_stored zeros_set gain0_loaded").split()]
        gate_row = [sem(f"gate_row{j}") for j in range(2)]

        chunks = chunks_of_layer(0) + chunks_of_layer(1) + chunks_of_block2()
        CL, NCH = len(chunks_of_layer(0)), len(chunks)
        arrive, slot_total = [], [0] * MSLOTS
        for n, c in enumerate(chunks):
            slot_total[n % SLOTS] += 16 * (3 if c[1] == "w_br" else 1)
            arrive.append((slot_full[n % SLOTS], slot_total[n % SLOTS]))

        def slot(n):
            return ring[:, n % SLOTS, :, :]

        bk = Banks(bank_full, bank_free)
        last_use = [None] * NCH
        for l in range(DEPTH):
            c0 = l * CL
            for k in range(KD):
                bk.give((l, "hT", k))
            for n, w in (("sq", 3), ("sk", 3), ("sv", 2), ("d", 2), ("iq", 2), ("ik", 2), ("hq", 4),
                         ("hf", 4), ("hi", 2), ("hg", 2)):
                for m in range(w):
                    bk.give((l, n, m))
                last_use[c0] = bk.full((l, n, w - 1))
                c0 += 1
            for s in MIX:
                if s[0] in ("g", "rt", "z", "u", "o", "ix", "hl", "hx", "ho", "oht"):
                    bk.give((l,) + s)
                    if s[0] == "g" and s[1] % 4 == 3:
                        last_use[c0] = bk.full((l,) + s)
                        c0 += 1
                elif s[0] in ("dl", "dt"):
                    bk.give((l, s[0], s[1], 0))
                elif s[0] == "dp" and s[1] % 4 == 0:
                    bk.give((l, "pair", s[1] // 4), long=True)
            for m in range(KD):
                bk.give((l, "yab", m))
                bk.give((l, "yh", m))
                if m % 4 == 3:
                    last_use[c0] = bk.full((l, "yh", m))
                    c0 += 1
            for n in range(2):
                for i in range(NT):
                    bk.give((l, "wo", n, i))
                last_use[c0] = bk.full((l, "wo", n, 1))
                c0 += 1
            for k in range(KD):
                bk.give((l, "h2T", k))
            for f in range(NF):
                bk.give((l, "up", f))
                if f % 4 == 3:
                    last_use[c0] = bk.full((l, "up", f))
                    c0 += 1
            for n in range(2):
                for i in range(NT):
                    bk.give((l, "down", n, i))
            for c in range(6):
                last_use[c0] = (down_chunk_used, 6 * l + c + 1)
                c0 += 1
            for n in range(2):
                last_use[c0] = bk.full((l, "down", n, 1))
                c0 += 1
            assert c0 == (l + 1) * CL

        class Attention:

            def __init__(self, tag, first, units, prb, prT, pair_out):
                self.tag, self.first, self.units = tag, first, units
                self.prb, self.prT, self.pair_out = prb, prT, pair_out

        dsa, upl = [], N_DSA * NT
        for l in range(DEPTH):
            units = []
            for u in range(upl):
                pair, i, hh = u // 4, (u // 2) % 2, u % 2
                units.append(([(RT[:, pair, :], RT[:, 3, :], negsel[:, i, :], [dv[:, kt, :] for kt in range(NT)])],
                              i, 64 * hh))
            dsa.append(Attention(l, l * upl, units, prb, prT, lambda pair: odT[:, pair, :]))
        units2 = []
        for pair in range(KD):
            for i in range(NT):
                for hh in range(2):
                    if pair < 4:
                        h, m0 = 2 * pair + hh, 2 - 2 * i
                        segs = [(PT[:, pair, :], PT[:, 4 + pair, :],
                                 na_bias[:, h, m0:m0 + 4, :].rearrange("p m c -> p (m c)"),
                                 [PP[:, kt, 1024 + 64 * h:1088 + 64 * h] for kt in range(NT)])]
                    elif pair < 6:
                        h, c0 = 2 * (pair - 4) + hh, P - P * i
                        segs = [(PT[:, 8 + 2 * g + pair - 4, :], PT[:, 14 + 2 * g + pair - 4, :],
                                 dil_bias[:, 4 * g + h, c0:c0 + T],
                                 [PP[:, kt, 3072 + 256 * g + 64 * h:3136 + 256 * g + 64 * h] for kt in range(NT)])
                                for g in range(DIL_G)]
                    else:
                        h = 2 * (pair - 6) + hh
                        segs = [(PT[:, 14 + pair, :], PT[:, 16 + pair, :], zero_bias,
                                 [kv[:, kt, 256 + 64 * h:320 + 64 * h] for kt in range(NT)])]
                    units2.append((segs, i, 64 * hh))
        att2 = Attention(2, DEPTH * upl, units2, prb2, prT2, oT2)
        ATT2_STEPS = attn_steps(len(units2))

        c0 = DEPTH * CL
        for g in range(DIL_G):
            bk.give((2, "t5", g))
        for k in range(KD):
            bk.give((2, "memT", k))
        for i in range(NT):
            bk.give((2, "kv", i))
        last_use[c0] = bk.full((2, "kv", 1))
        for k in range(KD):
            bk.give((2, "hT", k))
        for c in range(8):
            for i in range(NT):
                bk.give((2, "p", c, i))
            last_use[c0 + 1 + c] = bk.full((2, "p", c, 1))
        for c in range(24):
            bk.give((2, "pt", c))
        for s in ATT2_STEPS:
            if s[0] in ("dl", "dt"):
                for g in range(len(units2[s[1]][0])):
                    bk.give((2, s[0], s[1], g))
            elif s[0] == "dp" and s[1] % 4 == 0:
                bk.give((2, "pair", s[1] // 4), long=True)
        for n in range(2):
            for i in range(NT):
                bk.give((2, "wo", n, i))
            last_use[c0 + 9 + n] = bk.full((2, "wo", n, 1))
        for k in range(KD):
            bk.give((2, "h2T", k))
        for i in range(NT):
            bk.give((2, "router", i))
        bk.give((2, "gateT"))
        base = list(bk.uses)

        segments = [(kv, 0, 4, 5, 1.0, 0), (PP, 0, 8, 0, 0.125, 0), (PP, 512, 8, 1, 1.0, 1),
                    (PP, 1536, 12, 2, 0.125, 4), (PP, 2304, 12, 3, 1.0, 5), (PP, 3840, 4, 4, 0.125, 7)]
        tiles2 = [(PP, 128 * c) for c in range(8)] + [(PP, 1536 + 128 * c) for c in range(12)] + \
                 [(PP, 3840), (PP, 3968), (kv, 0), (kv, 128)]

        wo_done = [[bk.freed((l, "wo", n, i)) for n in range(2) for i in range(NT)] for l in range(3)]
        down_done = [[bk.freed((l, "down", n, i)) for n in range(2) for i in range(NT)] for l in range(DEPTH)]
        norms = [(x, [(x_loaded, 16)], xn, (0, "hT"), g_mix[:, 0, :], hT),
                 (x, wo_done[0], xn, (0, "h2T"), g_mlp[:, 0, :], hT),
                 (x, down_done[0], xn, (1, "hT"), g_mix[:, 1, :], hT),
                 (x, wo_done[1], xn, (1, "h2T"), g_mlp[:, 1, :], hT),
                 (xn2, [(mem_loaded, 16)], xn2, (2, "memT"), g_mem2, memT),
                 (x, down_done[1], xn2, (2, "hT"), g_mix2, hT),
                 (x, wo_done[2], xn3, (2, "h2T"), g_ffn2, hT)]

        block = ctx.enter_context(nc.Block())

        @block.sync
        def _(sp):
            sp.dma_start(x[:, :, :], a["x"].rearrange("b (i p) d -> p (b i) d", p=P)).then_inc(x_loaded, 16)
            sp.dma_start(cst[:, :], a["c_main"]).then_inc(consts_loaded, 16)
            for n, (l, name, r0, kt, c0, w) in enumerate(chunks):
                if n >= SLOTS:
                    sp.wait_ge(*last_use[n - SLOTS])
                s = slot(n)
                if name == "w_br":
                    k = 0
                    for part, kk in (("w_br_sb", 3), ("w_br_dsa", 3), ("w_br_hgrn", 2)):
                        src = a[part][l, :, c0:c0 + w].rearrange("(k p) n -> p k n", p=P)
                        sp.dma_start(s[:, k:k + kk, 0:w], src).then_inc(arrive[n][0], 16)
                        k += kk
                else:
                    src = a[name][l, r0:r0 + kt * P, c0:c0 + w].rearrange("(k p) n -> p k n", p=P)
                    sp.dma_start(s[:, 0:kt, 0:w], src).then_inc(arrive[n][0], 16)
            for n in range(NCH - SLOTS, NCH):
                sp.wait_ge(*last_use[n])
            sp.wait_ge(gate_stored, 16)
            with sp.Fori(0, N_EXP // 2) as it:
                for e in range(2):
                    ex = it * 2 + e
                    sp.wait_ge(y_step, it * 2 + (e + 1))
                    sp.dma_start(gate[e], gate_dram[bass.ds(ex, 1), :].broadcast_to([P, T])
                                 ).then_inc(gate_row[e], 16)
                    for j, name in enumerate(("w1_2", "w3_2", "w2_2")):
                        q = 3 * e + j
                        src = a[name][0, bass.ds(ex, 1), :, :].rearrange("e (k p) n -> p (e k) n", p=P)
                        dst = wslot[q]
                        if j == 2:
                            dst = dst.rearrange("p k n -> p (k n)").rearrange("p (k n) -> p k n", k=4)
                        sp.dma_start(dst, src).then_inc(slot_full[q], 16)

        n_params = [0]

        @block.gpsimd
        def _(pool):
            def col(dst, src):
                pool.dma_start(dst, src.rearrange("(k p) -> p k", p=P)).then_inc(params_loaded, 16)
                n_params[0] += 16

            def row(dst, src, w):
                pool.dma_start(dst, src.unsqueeze(0).broadcast_to([P, w])).then_inc(params_loaded, 16)
                n_params[0] += 16

            pool.dma_start(g_mix[:, 0, :], a["norm_mix"][0].rearrange("(k p) -> p k", p=P)).then_inc(gain0_loaded, 16)
            for l in range(DEPTH):
                if l:
                    col(g_mix[:, l, :], a["norm_mix"][l])
                col(g_mlp[:, l, :], a["norm_mlp"][l])
                col(lbraw[:, l, :], a["hgrn_lb"][l])
                row(qn[:, l, :], a["qn_dsa"][l], HD)
                row(kn[:, l, :], a["kn_dsa"][l], HD)
                row(onorm[:, l, :], a["hgrn_onorm"][l], HD)
            col(g_mix2, a["g_mix_2"][0])
            col(g_mem2, a["g_mem_2"][0])
            col(g_ffn2, a["g_ffn_2"][0])
            for j in range(6):
                row(qkg[:, j, :], a["qk_gain_2"][0, j // 2, j % 2], HD)
            row(rbias[:, 0:N_GRP], a["b_r1_2"][0], N_GRP)
            row(rbias[:, N_GRP:36], a["b_r2_2"][0], N_EXP)
            for dst, name in ((wr[:, :, 0:N_GRP], "w_r1_2"), (wr[:, :, N_GRP:36], "w_r2_2")):
                pool.dma_start(dst, a[name][0].rearrange("(k p) n -> p k n", p=P)).then_inc(params_loaded, 16)
                n_params[0] += 16
            for w in down_done[DEPTH - 1]:
                pool.wait_ge(*w)
            pool.dma_start(xn2, a["mem_2"].rearrange("b (i p) d -> p (b i) d", p=P)).then_inc(mem_loaded, 16)
            pool.dma_start(t5_onehot, a["c_t5"]).then_inc(t5_loaded, 16)
            pool.dma_start(t5_mask, a["c_t5m"]).then_inc(t5_loaded, 16)
            pool.dma_start(t5_tab, a["t5_table_2"]).then_inc(t5_loaded, 16)
            rows, cols = 15, 31
            pool.dma_start(na_dram, a["na_rpb_2"].rearrange("l h r c -> l (h r c)").broadcast_to([GRID, NA_ROW])
                           ).then_inc(na_stored, 16)
            pool.wait_ge(na_stored, 16)
            for r in range(2):
                for h in range(NA_HEADS):
                    src = bass.AP(tensor=na_dram.tensor, offset=(h * rows + 5 - r) * cols + 15,
                                  ap=[[NA_ROW - 1, GRID], [cols, 6], [1, GRID]])
                    pool.dma_start(na_bias[64 * r:64 * r + 64, h, :, :], src).then_inc(bias_loaded, 16)
            pool.wait_ge(t5_masked, DIL_G)
            for g in range(DIL_G):
                pool.dma_start(t5_dram[4 * g:4 * g + 4, :, :],
                               t5_rows[:, 512 * g:512 * g + 512].unsqueeze(1).broadcast_to([4, P, 512])
                               ).then_inc(t5_stored, 16)
            pool.wait_ge(t5_stored, 16 * DIL_G)
            for h in range(12):
                src = bass.AP(tensor=t5_dram.tensor, offset=h * P * 512 + 127, ap=[[511, P], [1, 384]])
                pool.dma_start(dil_bias[:, h, :], src).then_inc(bias_loaded, 16)
            pool.wait_ge(gateT_ready, 1)
            pool.dma_start(gate_dram, gateT[0:N_EXP, :]).then_inc(gate_stored, 16)
            for i in range(NT):
                pool.wait_ge(out_ready, 2 * (i + 1))
                pool.dma_start(out.rearrange("b (i p) d -> p (b i) d", p=P)[:, i, :], x[:, i, :]
                               ).then_inc(out_stored, 16)
            pool.wait_ge(out_stored, 16 * NT)

        BIASES = 16 * (2 * NA_HEADS + 12)
        GATES_IN_LOOP = N_EXP // 2

        @block.tensor
        def _(pe):
            mm, turn = nc.tensor.matmul, nc.tensor.transpose

            def bank_of(key):
                if bk.at[key][1]:
                    pe.wait_ge(*bk.before(key))
                return psum[bk.bank(key)]

            def full(ins, key):
                ins.then_inc(bank_full[bk.bank(key)], 1)

            def arrived(n):
                pe.wait_ge(*arrive[n])
                return slot(n)

            def wait_freed(keys):
                for k in keys:
                    pe.wait_ge(*bk.freed(k))

            def turn_rows(n):
                _, _, src, (l, name), _, _ = norms[n]
                pe.wait_ge(rows_normed, 2 * (n + 1))
                for k in range(KD):
                    b = bank_of((l, name, k))
                    for i in range(NT):
                        t = turn(b[:, i * P:(i + 1) * P], src[:, i, k * P:(k + 1) * P], ident)
                    full(t, (l, name, k))
                wait_freed([(l, name, k) for k in range(KD)])

            def feature_major(key, w, act):
                b = bank_of(key)
                for k in range(KD):
                    t = mm(b[:, 0:T], w[:, k, :], act[:, k, :], start=(k == 0), stop=(k == KD - 1))
                full(t, key)

            def token_major(key, w, act, i):
                b, cols = bank_of(key), w.shape[2]
                for k in range(KD):
                    t = mm(b[:, 0:cols], act(k)[:, i * P:(i + 1) * P], w[:, k, :],
                           start=(k == 0), stop=(k == KD - 1))
                full(t, key)

            def h_tile(k):
                return hT[:, k, :]

            def attention(at, kind, u):
                segs, i, b0 = at.units[u]
                U = at.first + u
                if kind == "dl":
                    for g, (q, kk, _, _) in enumerate(segs):
                        b = bank_of((at.tag, "dl", u, g))
                        t = mm(b[:, 0:T], q[b0:b0 + 64, i * P:(i + 1) * P], kk[b0:b0 + 64, :], start=True, stop=True)
                        full(t, (at.tag, "dl", u, g))
                elif kind == "dt":
                    pe.wait_ge(probs_ready, U + 1)
                    for g in range(len(segs)):
                        b = bank_of((at.tag, "dt", u, g))
                        for kt in range(NT):
                            c = T * g + P * kt
                            t = turn(b[:, kt * P:(kt + 1) * P], at.prb[U % 4][:, c:c + P], ident)
                        full(t, (at.tag, "dt", u, g))
                elif kind == "dp":
                    key = (at.tag, "pair", u // 4)
                    b = bank_of(key) if u % 4 == 0 else psum[bk.bank(key)]
                    wait_freed([(at.tag, "dt", u, g) for g in range(len(segs))])
                    n = 0
                    for g, (_, _, _, v) in enumerate(segs):
                        for kt in range(NT):
                            t = mm(b[b0:b0 + 64, i * P:(i + 1) * P], v[kt], at.prT[U % 3][:, NT * g + kt, :],
                                   start=(n == 0), stop=(n == NT * len(segs) - 1))
                            n += 1
                    t.then_inc(probsT_used, 1)

            pe.wait_ge(consts_loaded, 16)
            for l in range(DEPTH):
                c0 = l * CL
                turn_rows(2 * l)
                for c, name in ((0, "sq"), (1, "sk")):
                    w = arrived(c0 + c)
                    for m in range(3):
                        feature_major((l, name, m), w[:, :, P * m:P * m + P], hT)
                for c, name, cols in ((2, "sv", 384), (3, "d", 512), (4, "iq", 512), (5, "ik", 72)):
                    w = arrived(c0 + c)
                    for i in range(NT):
                        token_major((l, name, i), w[:, :, 0:cols], h_tile, i)
                for c, name in ((6, "hq"), (7, "hf")):
                    w = arrived(c0 + c)
                    for m in range(4):
                        feature_major((l, name, m), w[:, :, P * m:P * m + P], hT)
                for c, name in ((8, "hi"), (9, "hg")):
                    w = arrived(c0 + c)
                    for i in range(NT):
                        token_major((l, name, i), w[:, :, 0:T], h_tile, i)

                for s in MIX:
                    kind, key = s[0], (l,) + s
                    if kind == "g":
                        m = s[1]
                        w = arrived(c0 + 10 + m // 4)
                        feature_major(key, w[:, :, P * (m % 4):P * (m % 4) + P], hT)
                    elif kind == "rt":
                        pe.wait_ge(R_ready, l + 1)
                        b, c = bank_of(key), s[1]
                        for i in range(NT):
                            t = turn(b[:, i * P:(i + 1) * P], R[:, i, 2 * c:2 * c + 2, :].rearrange("p h d -> p (h d)"),
                                     ident)
                        full(t, key)
                    elif kind in ("z", "u"):
                        h = s[1]
                        r = slice(64 * (h % 2), 64 * (h % 2) + 64)
                        q, kk = sqT[r, h // 2, :], skT[r, h // 2, :]
                        if h == 0:
                            wait_freed([(l, n, m) for n in ("sq", "sk") for m in range(3)])
                        if kind == "z":
                            b = bank_of(key)
                            mm(b[:, 0:T], kk[:, 0:P], q, start=True, stop=True)
                            t = mm(b[:, T:T + P], kk[:, P:T], q[:, P:T], start=True, stop=True)
                        else:
                            pe.wait_ge(sp_ready, l * N_SB + h + 1)
                            b, L = bank_of(key), sbL[h % 2]
                            mm(b[:, 0:P], kk[:, 0:P], q[:, 0:P], start=True, stop=False)
                            mm(b[:, 0:P], negtri, L[:, 0:P], start=False, stop=True)
                            mm(b[:, P:T], kk[:, 0:P], q[:, P:T], start=True, stop=False)
                            mm(b[:, P:T], negtri, L[:, P:T], start=False, stop=False)
                            mm(b[:, P:T], negones, L[:, T:T + P], start=False, stop=True)
                            mm(b[:, T:T + P], kk[:, P:T], q[:, P:T], start=True, stop=False)
                            t = mm(b[:, T:T + P], negtri, L[:, T:T + P], start=False, stop=True)
                        full(t, key)
                    elif kind == "o":
                        pr = s[1]
                        if pr == 0:
                            wait_freed([(l, "sv", 0), (l, "sv", 1)])
                        pe.wait_ge(sba_ready, l * N_SB + 2 * pr + 2)
                        b = bank_of(key)
                        for hh in range(2):
                            h = 2 * pr + hh
                            w_, o_ = sbA[h % 4], b[64 * hh:64 * hh + 64, :]
                            mm(o_[:, 0:P], sv[:, 0, HD * h:HD * h + HD], w_[:, 0:P], start=True, stop=True)
                            mm(o_[:, P:T], sv[:, 0, HD * h:HD * h + HD], w_[:, P:T], start=True, stop=False)
                            t = mm(o_[:, P:T], sv[:, 1, HD * h:HD * h + HD], w_[:, T:T + P], start=False, stop=True)
                        full(t, key)
                    elif kind == "ix":
                        i, j = s[1], s[2]
                        if i == 0 and j == 0:
                            wait_freed([(l, "rt", c) for c in range(9)])
                        r, b = slice(64 * (j % 2), 64 * (j % 2) + 64), bank_of(key)
                        t = mm(b[:, 0:T], RT[r, 4 + j // 2, i * P:(i + 1) * P], RT[r, 8, :], start=True, stop=True)
                        full(t, key)
                    elif kind == "hx":
                        pe.wait_ge(level_ready, l * 8 + 1)
                        b = bank_of(key)
                        for h in range(N_HG):
                            t = mm(b[:, P * h:P * h + P], E[0][:, h, 0:P], E[0][:, h, P:T], start=True, stop=True)
                        full(t, key)
                    elif kind == "hl":
                        j, hp = s[1], s[2]
                        if j < 8:
                            pe.wait_ge(level_ready, l * 8 + j + 1)
                        b = bank_of(key)
                        for h in range(2):
                            for i in range(NT):
                                hh, lo, c = 2 * hp + h, i * P, P * (2 * h + i)
                                left = (E[j % 2] if j < 8 else kT)[:, hh, lo:lo + P]
                                right = (E[j % 2] if j < 8 else hqT)[:, hh, lo:lo + P]
                                t = mm(b[:, c:c + P], left, right, start=True, stop=True)
                        full(t, key)
                    elif kind == "ho":
                        wait_freed([(l, "hi", 0), (l, "hi", 1), (l, "hx"), (l, "hl", 8, 0), (l, "hl", 8, 1)])
                        b = bank_of(key)
                        for h in range(N_HG):
                            v0, v1 = hv[:, 0, HD * h:HD * h + HD], hv[:, 1, HD * h:HD * h + HD]
                            o0, o1 = b[:, HD * h:HD * h + HD], b[:, T + HD * h:T + HD * h + HD]
                            mm(o0, attT[:, h, 0, :], v0, start=True, stop=True)
                            mm(o1, attX[:, h, :], v0, start=True, stop=False)
                            t = mm(o1, attT[:, h, 1, :], v1, start=False, stop=True)
                        full(t, key)
                    elif kind == "oht":
                        pe.wait_ge(og_ready, l + 1)
                        b = bank_of(key)
                        for i in range(NT):
                            t = turn(b[:, i * P:(i + 1) * P],
                                     og[:, 4 * i + 2 * s[1]:4 * i + 2 * s[1] + 2, :].rearrange("p h d -> p (h d)"),
                                     ident)
                        full(t, key)
                    elif kind in ("dl", "dt", "dp"):
                        attention(dsa[l], kind, s[1])
                wait_freed([(l, "o", pr) for pr in range(3)] + [(l, "pair", pr) for pr in range(3)] +
                           [(l, "oht", f) for f in range(2)])
                for m in range(KD):
                    w = arrived(c0 + 16 + m // 4)[:, :, P * (m % 4):P * (m % 4) + P]
                    b = bank_of((l, "yab", m))
                    for k in range(3):
                        mm(b[:, 0:T], w[:, k, :], osT[:, k, :], start=(k == 0), stop=(k == 2))
                    for k in range(3):
                        t = mm(b[:, T:2 * T], w[:, 3 + k, :], odT[:, k, :], start=(k == 0), stop=(k == 2))
                    full(t, (l, "yab", m))
                    b = bank_of((l, "yh", m))
                    for k in range(2):
                        t = mm(b[:, 0:T], w[:, 6 + k, :], ohT[:, k, :], start=(k == 0), stop=(k == 1))
                    full(t, (l, "yh", m))
                pe.wait_ge(mix_ready, KD * (l + 1))
                for n in range(2):
                    w = arrived(c0 + 18 + n)
                    for i in range(NT):
                        token_major((l, "wo", n, i), w, lambda k: mixT[:, k, :], i)
                turn_rows(2 * l + 1)
                for f in range(NF):
                    w = arrived(c0 + 20 + f // 4)
                    feature_major((l, "up", f), w[:, :, P * (f % 4):P * (f % 4) + P], hT)
                for kb in range(4):
                    for n in range(2):
                        w = arrived(c0 + 28 + 2 * kb + n)
                        for i in range(NT):
                            key = (l, "down", n, i)
                            b = bank_of(key) if kb == 0 else psum[bk.bank(key)]
                            for k in range(KD):
                                pe.wait_ge(hid_ready, NF * l + 8 * kb + k + 1)
                                t = mm(b[:, :], hid[:, 8 * kb + k, i * P:(i + 1) * P], w[:, k, :],
                                       start=(kb == 0 and k == 0), stop=(kb == 3 and k == KD - 1))
                            if kb == 3:
                                full(t, key)
                            elif i == NT - 1:
                                t.then_inc(down_chunk_used, 1)

            c0 = DEPTH * CL
            pe.wait_ge(t5_loaded, 48)
            for g in range(DIL_G):
                b = bank_of((2, "t5", g))
                t = mm(b[0:4, :], t5_tab[:, 4 * g:4 * g + 4], t5_onehot[:, 512 * g:512 * g + 512], start=True, stop=True)
                full(t, (2, "t5", g))
            turn_rows(4)
            w = arrived(c0)
            for i in range(NT):
                token_major((2, "kv", i), w, lambda k: memT[:, k, :], i)
            turn_rows(5)
            for c in range(8):
                w = arrived(c0 + 1 + c)
                for i in range(NT):
                    token_major((2, "p", c, i), w, h_tile, i)
            pe.wait_ge(seg_normed, len(segments))
            for c, (buf, col) in enumerate(tiles2):
                b = bank_of((2, "pt", c))
                for i in range(NT):
                    t = turn(b[:, i * P:(i + 1) * P], buf[:, i, col:col + P], ident)
                full(t, (2, "pt", c))
            wait_freed([(2, "pt", c) for c in range(24)])
            wait_freed([(2, "p", c, i) for c in range(8) for i in range(NT)])
            for kind, u in ATT2_STEPS:
                attention(att2, kind, u)
            wait_freed([(2, "pair", pr) for pr in range(KD)])
            for n in range(2):
                w = arrived(c0 + 9 + n)
                for i in range(NT):
                    token_major((2, "wo", n, i), w, oT2, i)
            turn_rows(6)
            for i in range(NT):
                token_major((2, "router", i), wr, h_tile, i)
            pe.wait_ge(gates_made, 1)
            b = bank_of((2, "gateT"))
            for i in range(NT):
                t = turn(b[0:N_EXP, i * P:(i + 1) * P], fine[5][:, i, :], ident)
            full(t, (2, "gateT"))
            for q in range(4):
                pe.wait_ge(bank_free[4 + q], base[4 + q])
                i, n = q // 2, q % 2
                t = mm(psum[4 + q][:, :], ident, x[:, i, 512 * n:512 * n + 512], start=True, stop=False)
                if q >= 2:
                    t.then_inc(y_step, 1)
            with pe.Fori(0, N_EXP // 2) as it:
                for e in range(2):
                    pe.wait_ge(slot_full[3 * e], it * 16 + (slot_total[3 * e] + 16))
                    pe.wait_ge(slot_full[3 * e + 1], it * 16 + (slot_total[3 * e + 1] + 16))
                    for m in range(4):
                        pe.wait_ge(bank_free[m], it * 2 + (base[m] + e))
                        for j in range(2):
                            for k in range(KD):
                                t = mm(psum[m][:, T * j:T * j + T], wslot[3 * e + j][:, k, P * m:P * m + P],
                                       hT[:, k, :], start=(k == 0), stop=(k == KD - 1))
                        t.then_inc(bank_full[m], 1)
                    pe.wait_ge(slot_full[3 * e + 2], it * 16 + (slot_total[3 * e + 2] + 16))
                    w2 = wslot[3 * e + 2].rearrange("p k n -> p (k n)").rearrange("p (k n) -> p k n", k=4)
                    for k in range(4):
                        pe.wait_ge(aT_ready, it * 8 + (4 * e + k + 1))
                        for q in range(4):
                            i, n = q // 2, q % 2
                            t = mm(psum[4 + q][:, :], aT[e][:, k, i * P:(i + 1) * P], w2[:, k, 512 * n:512 * n + 512],
                                   start=False, stop=False)
                    t.then_inc(y_step, 1)
            pe.wait_ge(zeros_set, 1)
            for q in range(4):
                i, n = q // 2, q % 2
                t = mm(psum[4 + q][:, :], zeros, x[:, i, 512 * n:512 * n + 512], start=False, stop=True)
            t.then_inc(y_step, 1)

        @block.scalar
        def _(act):
            A_ = nc.scalar.activation
            steps = [0]

            def link(ins):
                ins.then_inc(act_step, 1)
                steps[0] += 1
                act.wait_ge(act_step, steps[0])

            def read(key):
                act.wait_ge(*bk.full(key))
                return psum[bk.bank(key)]

            def free(ins, key):
                ins.then_inc(bank_free[bk.bank(key)], 1)

            def norm(n):
                src, waits, rows, (l, name), gain, dst = norms[n]
                for w in waits:
                    act.wait_ge(*w)
                for i in range(NT):
                    junk = memT_flat[:, D * i:D * i + D] if n == 4 else rows[:, i, :]
                    t = A_(junk, src[:, i, :], ACT.Square, accum_out=ss[:, i:i + 1])
                link(t)
                A_(sd, ss, ACT.Sqrt, bias=eps_c, scale=1.0 / D).then_inc(std_ready, 1)
                act.wait_ge(gain0_loaded, 16)
                if n:
                    act.wait_ge(params_loaded, n_params[0])
                for k in range(0, KD, 2):
                    free(A_(dst[:, k, :], read((l, name, k))[:, 0:T], ACT.Copy, scale=gain[:, k:k + 1]), (l, name, k))

            def attention(at, kind, u):
                segs, i, b0 = at.units[u]
                U = at.first + u
                if kind == "dl":
                    act.wait_ge(rowmax_ready, U + 1)
                    p = at.prb[U % 4][:, 0:T * len(segs)]
                    A_(p, p, ACT.Exp, bias=nmax[:, U % 4:U % 4 + 1], accum_out=esum[:, U % 4:U % 4 + 1]
                       ).then_inc(exps_ready, 1)
                elif kind == "dt":
                    if U >= 3:
                        act.wait_ge(probsT_used, U - 2)
                    for g in range(len(segs)):
                        key = (at.tag, "dt", u, g)
                        src = read(key)[:, 0:T].rearrange("p (s t) -> p s t", s=NT)
                        free(A_(at.prT[U % 3][:, NT * g:NT * g + NT, :], src, ACT.Copy), key)
                elif kind == "dp" and u % 4 == 3:
                    act.wait_ge(probsT_used, U + 1)
                    key = (at.tag, "pair", u // 4)
                    free(A_(at.pair_out(u // 4), psum[bk.bank(key)][:, 0:T], ACT.Copy), key)

            act.wait_ge(eps_set, 1)
            for l in range(DEPTH):
                norm(2 * l)
                if l == 0:
                    act.wait_ge(lb_shifted, 1)
                    A_(lb_e, lb_e, ACT.Exp).then_inc(lb_exps, 1)
                for m in range(3):
                    free(A_(skT[:, m, :], read((l, "sk", m))[:, 0:T], ACT.Copy), (l, "sk", m))
                for i in range(NT):
                    free(A_(sv[:, i, :], read((l, "sv", i))[:, 0:384], ACT.Copy), (l, "sv", i))
                for i in range(NT):
                    b = read((l, "d", i))
                    A_(R[:, i, 0:7, :], b[:, 0:448].rearrange("p (h d) -> p h d", h=7), ACT.Copy)
                    free(A_(dv[:, i, :], b[:, 448:512], ACT.Copy), (l, "d", i))
                for i in range(NT):
                    b = read((l, "iq", i))
                    free(A_(R[:, i, 8:16, :], b[:, :].rearrange("p (h d) -> p h d", h=8), ACT.Copy), (l, "iq", i))
                for i in range(NT):
                    b = read((l, "ik", i))
                    A_(R[:, i, 16, :], b[:, 0:HD], ACT.Copy)
                    A_(R[:, i, 17, :], b[:, 0:HD], ACT.Copy)
                    free(A_(iw[:, i, :], b[:, HD:HD + N_IDX], ACT.Copy, scale=IDX_SCALE), (l, "ik", i))
                act.wait_ge(head_sums, l + 1)
                A_(sd14, ss14, ACT.Sqrt, bias=eps_c, scale=1.0 / HD).then_inc(head_std, 1)
                for m in range(4):
                    if m >= 2:
                        act.wait_ge(*bk.freed((l, "hq", m - 2)))
                    A_(hsg[m % 2], read((l, "hq", m))[:, 0:T], ACT.Sigmoid).then_inc(sig_ready, 1)
                for m in range(4):
                    free(A_(fT[:, m, :], read((l, "hf", m))[:, 0:T], ACT.Sigmoid), (l, "hf", m))
                for i in range(NT):
                    free(A_(hv[:, i, :], read((l, "hi", i))[:, 0:T], ACT.Copy), (l, "hi", i))
                for i in range(NT):
                    act.wait_ge(*bk.freed((l, "hq", 2 + i)))
                    A_(hsg[i], read((l, "hg", i))[:, 0:T], ACT.Sigmoid).then_inc(sig_ready, 1)
                for s in MIX:
                    kind, key = s[0], (l,) + s
                    if kind == "g":
                        free(A_(gT[:, s[1], :], read(key)[:, 0:T], ACT.Copy), key)
                    elif kind == "rt" and s[1] % 2 == 0:
                        free(A_(RT[:, s[1], :], read(key)[:, 0:T], ACT.Copy), key)
                    elif kind == "z":
                        h = s[1]
                        if h >= 2:
                            act.wait_ge(*bk.full((l, "u", h - 2)))
                        L = sbL[h % 2]
                        link(A_(L, read(key)[:, 0:384], ACT.Abs))
                        link(A_(L, L, ACT.Exp, scale=-1.0))
                        A_(L, L, ACT.Ln, bias=1.0).then_inc(log1p_ready, 1)
                    elif kind == "u":
                        act.wait_ge(*bk.freed(key))
                        w_ = sbA[s[1] % 4]
                        A_(w_, w_, ACT.Exp).then_inc(sba_ready, 1)
                    elif kind == "o":
                        free(A_(osT[:, s[1], :], read(key)[:, 0:T], ACT.Copy), key)
                    elif kind == "hp":
                        act.wait_ge(f_ready, l + 1)
                        A_(fT, fT, ACT.Ln).then_inc(logf_ready, 1)
                    elif kind == "ix":
                        n = l * 16 + 8 * s[1] + s[2]
                        if n >= 2:
                            act.wait_ge(rel_used, n - 1)
                        free(A_(rel[n % 2], read(key)[:, 0:T], ACT.Relu), key)
                    elif kind == "lv":
                        act.wait_ge(level_exponents, l * 8 + s[1] + 1)
                        e = E[s[1] % 2]
                        A_(e, e, ACT.Exp).then_inc(level_exps, 1)
                    elif kind == "hx":
                        free(A_(attX, read(key)[:, :].rearrange("p (h t) -> p h t", h=N_HG), ACT.Copy), key)
                    elif kind == "ho":
                        free(A_(og, read(key)[:, :].rearrange("p (h d) -> p h d", h=8), ACT.Copy), key)
                    elif kind == "on":
                        act.wait_ge(o_sums, l + 1)
                        A_(sd8, ss8, ACT.Sqrt, bias=eps_c, scale=1.0 / HD).then_inc(o_std, 1)
                    elif kind == "oht":
                        free(A_(ohT[:, s[1], :], read(key)[:, 0:T], ACT.Copy), key)
                    elif kind in ("dl", "dt", "dp"):
                        attention(dsa[l], kind, s[1])
                for m in range(24):
                    act.wait_ge(*bk.freed((l, "g", m)))
                A_(gT, gT, ACT.Sigmoid).then_inc(gates_ready, 1)
                norm(2 * l + 1)
                for f in range(NF):
                    if NF * l + f >= 4:
                        act.wait_ge(hid_ready, NF * l + f - 3)
                    free(A_(hrl[f % 4], read((l, "up", f))[:, 0:T], ACT.Relu), (l, "up", f))

            norm(4)
            for i in range(NT):
                free(A_(kv[:, i, :], read((2, "kv", i))[:, :], ACT.Copy), (2, "kv", i))
            norm(5)

            def seg_square(j):
                buf, col, nh, g, sc, c = segments[j]
                w = nh * HD
                for i in range(NT):
                    keys = [(2, "kv", i)] if buf is kv else \
                        [(2, "p", cc, i) for cc in range(col // 512, (col + w - 1) // 512 + 1)]
                    for k in keys:
                        act.wait_ge(*bk.freed(k))
                if j >= 1:
                    act.wait_ge(seg_sums, j)
                src = buf[:, :, col:col + w]
                dst = squares[:, 0:NT * w].rearrange("p (i f) -> p i f", i=NT)
                A_(dst, src, ACT.Square).then_inc(seg_squared, 1)

            def seg_sqrt(j):
                nh = segments[j][2]
                act.wait_ge(seg_sums, j + 1)
                A_(seg_sd[:, :, 0:nh], seg_ss[:, :, 0:nh], ACT.Sqrt, bias=eps_c, scale=1.0 / HD).then_inc(seg_std, 1)

            seg_square(0)
            seg_sqrt(0)
            for c in range(8):
                if c % 2 == 0:
                    for i in range(NT):
                        free(A_(PP[:, i, 512 * c:512 * c + 512], read((2, "p", c, i))[:, :], ACT.Copy), (2, "p", c, i))
                for j in range(1, len(segments)):
                    if segments[j][5] == c:
                        seg_square(j)
                        seg_sqrt(j)
            for c in range(0, 24, 2):
                free(A_(PT[:, c, :], read((2, "pt", c))[:, 0:T], ACT.Copy), (2, "pt", c))
            for kind, u in ATT2_STEPS:
                attention(att2, kind, u)
            norm(6)
            act.wait_ge(router_shifted, 1)
            A_(grp[1], grp[1], ACT.Exp)
            A_(one[4], one[4], ACT.Exp).then_inc(router_exps, 1)
            with act.Fori(0, N_EXP // 2) as it:
                for e in range(2):
                    for m in range(4):
                        g = 4 * e + m
                        if m >= 2:
                            act.wait_ge(bank_free[m - 2], it * 2 + (base[m - 2] + e + 1))
                        else:
                            act.wait_ge(bank_free[m + 2], it * 2 + (base[m + 2] + e))
                        act.wait_ge(bank_full[m], it * 2 + (base[m] + e + 1))
                        A_(sgm[m % 2], psum[m][:, 0:T], ACT.Sigmoid).then_inc(sig2_ready, 1)

        @block.vector
        def _(dve):
            V = nc.vector
            steps = [0]

            def link(ins):
                ins.then_inc(dve_step, 1)
                steps[0] += 1
                dve.wait_ge(dve_step, steps[0])

            def read(key):
                dve.wait_ge(*bk.full(key))
                return psum[bk.bank(key)]

            def free(ins, key):
                ins.then_inc(bank_free[bk.bank(key)], 1)

            def own(key):
                dve.wait_ge(*bk.freed(key))

            def bc(ap, dims):
                return ap.broadcast_to([P] + dims)

            def norm(n):
                src, waits, rows, (l, name), gain, dst = norms[n]
                dve.wait_ge(std_ready, n + 1)
                link(V.reciprocal(rstd, sd))
                for i in range(NT):
                    V.tensor_scalar(rows[:, i, :], src[:, i, :], rstd[:, i:i + 1], None, ALU.mult
                                    ).then_inc(rows_normed, 1)
                dve.wait_ge(gain0_loaded, 16)
                if n:
                    dve.wait_ge(params_loaded, n_params[0])
                for k in range(1, KD, 2):
                    free(V.tensor_scalar(dst[:, k, :], read((l, name, k))[:, 0:T], gain[:, k:k + 1], None, ALU.mult),
                         (l, name, k))

            def attention(at, kind, u):
                segs, i, b0 = at.units[u]
                U, p = at.first + u, at.prb[(at.first + u) % 4]
                if kind == "dl":
                    if u >= 4:
                        for g in range(len(at.units[u - 4][0])):
                            dve.wait_ge(*bk.full((at.tag, "dt", u - 4, g)))
                    if U >= 4:
                        dve.wait_ge(exps_ready, U - 3)
                    for g, (_, _, bias, _) in enumerate(segs):
                        key = (at.tag, "dl", u, g)
                        free(V.tensor_tensor_reduce(out=p[:, T * g:T * g + T], in0=read(key)[:, 0:T], in1=bias,
                                                    scale=1.0, scalar=-3.0e38, op0=ALU.add, op1=ALU.max,
                                                    accum_out=mx[:, U % 4, g:g + 1]), key)
                    for g in range(len(segs)):
                        own((at.tag, "dl", u, g))
                    V.tensor_reduce(nmax[:, U % 4:U % 4 + 1], mx[:, U % 4, 0:len(segs)], AX.X, ALU.max, negate=True
                                    ).then_inc(rowmax_ready, 1)
                elif kind == "dn":
                    dve.wait_ge(exps_ready, U + 1)
                    link(V.reciprocal(rsum[:, U % 4:U % 4 + 1], esum[:, U % 4:U % 4 + 1]))
                    w = T * len(segs)
                    V.tensor_scalar(p[:, 0:w], p[:, 0:w], rsum[:, U % 4:U % 4 + 1], None, ALU.mult
                                    ).then_inc(probs_ready, 1)

            V.memset(eps_c, EPS).then_inc(eps_set, 1)
            dve.wait_ge(consts_loaded, 16)

            def lower_bounds():
                dve.wait_ge(params_loaded, n_params[0])
                link(V.tensor_tensor(lb_m, lbraw[:, 0, :], lbraw[:, 1, :], ALU.max))
                for l in range(DEPTH):
                    t = V.tensor_tensor(lb_e[:, l, :], lbraw[:, l, :], lb_m, ALU.subtract)
                t.then_inc(lb_shifted, 1)
                dve.wait_ge(lb_exps, 1)
                link(V.tensor_tensor(lb_s, lb_e[:, 0, :], lb_e[:, 1, :], ALU.add))
                link(V.reciprocal(lb_r, lb_s))
                for l in range(DEPTH):
                    t = V.tensor_tensor(lb_e[:, l, :], lb_e[:, l, :], lb_r, ALU.mult)
                link(t)
                V.tensor_tensor(lb[:, 0, :], lb_e[:, 0, :], lb_e[:, 0, :], ALU.subtract)
                link(V.tensor_tensor(lb_s, lb_e[:, 0, :], lb_e[:, 1, :], ALU.add))
                link(V.tensor_tensor(lb[:, 1, :], lb_s, lb_e[:, 0, :], ALU.subtract))
                link(V.tensor_scalar(omlb, lb, -1.0, 1.0, ALU.mult, ALU.add))

            for l in range(DEPTH):
                norm(2 * l)
                if l == 0:
                    lower_bounds()
                for m in range(3):
                    free(V.tensor_scalar(sqT[:, m, :], read((l, "sq", m))[:, 0:T], HD ** -0.5, None, ALU.mult),
                         (l, "sq", m))
                for n in ("d", "iq", "ik"):
                    for i in range(NT):
                        dve.wait_ge(*bk.freed((l, n, i)))
                q7 = R[:, :, 0:7, :]
                for i in range(NT):
                    t = V.tensor_tensor(sq14[:, i], R[:, i, 0:7, :], R[:, i, 0:7, :], ALU.mult)
                link(t)
                V.tensor_reduce(ss14, sq14, AX.X, ALU.add).then_inc(head_sums, 1)
                for m in range(4):
                    dve.wait_ge(sig_ready, 6 * l + m + 1)
                    free(V.tensor_tensor(hqT[:, m, :], read((l, "hq", m))[:, 0:T], hsg[m % 2], ALU.mult), (l, "hq", m))
                dve.wait_ge(head_std, l + 1)
                link(V.reciprocal(r14, sd14))
                link(V.tensor_scalar(r14[:, :, 0:N_DSA], r14[:, :, 0:N_DSA], HD ** -0.5, None, ALU.mult))
                for i in range(NT):
                    t = V.tensor_tensor(R[:, i, 0:7, :], R[:, i, 0:7, :], bc(r14[:, i, :].unsqueeze(2), [7, HD]), ALU.mult)
                link(t)
                for i in range(NT):
                    V.tensor_tensor(R[:, i, 0:N_DSA, :], R[:, i, 0:N_DSA, :],
                                    bc(qn[:, l, :].unsqueeze(1), [N_DSA, HD]), ALU.mult)
                    t = V.tensor_tensor(R[:, i, 6, :], R[:, i, 6, :], kn[:, l, :], ALU.mult)
                link(t)
                link(V.tensor_copy(R[:, :, 7, :], R[:, :, 6, :]))
                a1 = ra[:, 0:288].rearrange("p (i h d) -> p i h d", i=NT, h=RH)
                a2 = ra[:, 288:576].rearrange("p (i h d) -> p i h d", i=NT, h=RH)
                a3 = ra[:, 576:864].rearrange("p (i h d) -> p i h d", i=NT, h=RH)
                x1, x2 = R[:, :, :, 0:8], R[:, :, :, 8:16]
                co = bc(cosT.unsqueeze(2), [NT, RH, 8])
                si = bc(sinT.unsqueeze(2), [NT, RH, 8])
                V.tensor_tensor(a1, x1, co, ALU.mult)
                V.tensor_tensor(a2, x2, si, ALU.mult)
                link(V.tensor_tensor(a3, x1, si, ALU.mult))
                link(V.tensor_tensor(x1, a1, a2, ALU.subtract))
                link(V.tensor_tensor(a1, x2, co, ALU.mult))
                V.tensor_tensor(x2, a1, a3, ALU.add).then_inc(R_ready, 1)
                for i in range(NT):
                    dve.wait_ge(sig_ready, 6 * l + 4 + i + 1)
                    free(V.tensor_tensor(hgs[:, i, :], read((l, "hg", i))[:, 0:T], hsg[i], ALU.mult), (l, "hg", i))

                for s in MIX:
                    kind, key = s[0], (l,) + s
                    if kind == "rt" and s[1] % 2 == 1:
                        free(V.tensor_copy(RT[:, s[1], :], read(key)[:, 0:T]), key)
                    elif kind == "z":
                        h, L = s[1], sbL[s[1] % 2]
                        dve.wait_ge(log1p_ready, l * N_SB + h + 1)
                        free(V.scalar_tensor_tensor(out=L, in0=read(key)[:, 0:384], scalar=0.0, in1=L,
                                                    op0=ALU.max, op1=ALU.add), key)
                        own(key)
                        V.tensor_tensor(L, L, sbmask, ALU.mult).then_inc(sp_ready, 1)
                    elif kind == "u":
                        h = s[1]
                        if h >= 4:
                            dve.wait_ge(*bk.full((l, "o", (h - 4) // 2)))
                        free(V.tensor_tensor(sbA[h % 4], read(key)[:, 0:384], sbneg, ALU.add), key)
                    elif kind == "hp":
                        for m in range(N_HG):
                            dve.wait_ge(*bk.freed((l, "hf", m)))
                            t = V.tensor_scalar(fT[:, m, :], fT[:, m, :], omlb[:, l, m:m + 1], lb[:, l, m:m + 1],
                                                ALU.mult, ALU.add)
                        link(t)
                        link(V.tensor_scalar(kT, fT, -1.0, 1.0, ALU.mult, ALU.add))
                        V.tensor_scalar(fT, fT, F_MIN, None, ALU.max).then_inc(f_ready, 1)
                        link(V.memset(attT, 0.0))
                        dve.wait_ge(logf_ready, l + 1)
                        for m in range(N_HG):
                            t = V.tensor_tensor_scan(bT[:, m, :], scan0, fT[:, m, :], 0.0, ALU.mult, ALU.add)
                        link(t)
                    elif kind == "ix":
                        i, j = s[1], s[2]
                        n = l * 16 + 8 * i + j
                        dve.wait_ge(*bk.freed(key))
                        if j == 0:
                            t = V.tensor_scalar(score[:, i, :], rel[n % 2], iw[:, i, 0:1], None, ALU.mult)
                        else:
                            t = V.scalar_tensor_tensor(out=score[:, i, :], in0=rel[n % 2], scalar=iw[:, i, j:j + 1],
                                                       in1=score[:, i, :], op0=ALU.mult, op1=ALU.add)
                        t.then_inc(rel_used, 1)
                        dve.wait_ge(rel_used, n + 1)
                    elif kind == "tk":
                        i = s[1]
                        sc, sel = score[:, i, :], negsel[:, i, :]
                        link(V.tensor_scalar(sel, causal[:, i, :], -1.0, -NEG, ALU.add, ALU.mult))
                        link(V.tensor_tensor(sc, sc, sel, ALU.add))
                        for _ in range(TOPK // 8):
                            link(V.max(out=top8, in_=sc))
                            link(V.match_replace(out=sc, in_to_replace=top8, in_values=sc, imm_value=-3.0e38))
                        link(V.tensor_scalar(sel, sc, -2.0e38, None, ALU.is_le))
                        link(V.tensor_tensor(sel, sel, causal[:, i, :], ALU.mult))
                        link(V.tensor_scalar(sel, sel, -1.0, -NEG, ALU.add, ALU.mult))
                    elif kind == "lv":
                        j, e = s[1], E[s[1] % 2]
                        if j < 2:
                            dve.wait_ge(*bk.full((l, "o", 2)))
                        elif j == 2:
                            dve.wait_ge(*bk.full((l, "hx")))
                        else:
                            dve.wait_ge(*bk.full((l, "hl", j - 2, 1)))
                        if j == 0:
                            b4 = bT.rearrange("p h (n c) -> p h n c", c=HG_CHUNK)
                            e4 = e.rearrange("p h (n c) -> p h n c", c=HG_CHUNK)
                            end = b4[:, :, :, HG_CHUNK - 1:HG_CHUNK]
                            link(V.tensor_tensor(e4[:, :, 0:2, :], bc(end[:, :, 0:2, :], [4, 2, HG_CHUNK]),
                                                 b4[:, :, 0:2, :], ALU.subtract))
                            V.tensor_tensor(e4[:, :, 0, :], e4[:, :, 0, :], bc(end[:, :, 1, :], [4, HG_CHUNK]), ALU.add)
                            V.tensor_copy(e4[:, :, 2, :], b4[:, :, 2, :])
                            t = V.tensor_tensor(e4[:, :, 3, :], b4[:, :, 3, :], bc(end[:, :, 2, :], [4, HG_CHUNK]), ALU.add)
                        else:
                            half = HG_CHUNK >> (j - 1)
                            m = N_HG * T // (2 * half)
                            bv = bT.rearrange("p h t -> p (h t)").rearrange("p (m s c) -> p m s c", s=2, c=half)
                            ev = e.rearrange("p h t -> p (h t)").rearrange("p (m s c) -> p m s c", s=2, c=half)
                            end = bc(bv[:, :, 0, half - 1:half], [m, half])
                            V.tensor_tensor(ev[:, :, 0, :], end, bv[:, :, 0, :], ALU.subtract)
                            if j == 1:
                                t = V.tensor_copy(ev[:, :, 1, :], bv[:, :, 1, :])
                            else:
                                t = V.tensor_tensor(ev[:, :, 1, :], bv[:, :, 1, :], end, ALU.subtract)
                        t.then_inc(level_exponents, 1)
                    elif kind == "lm":
                        j, e = s[1], E[s[1] % 2]
                        half = P if j == 0 else HG_CHUNK >> (j - 1)
                        dve.wait_ge(level_exps, l * 8 + j + 1)
                        ev, kv_, qv_ = [z.rearrange("p h t -> p (h t)").rearrange("p (m s c) -> p m s c", s=2, c=half)
                                        for z in (e, kT, hqT)]
                        V.tensor_tensor(ev[:, :, 0, :], ev[:, :, 0, :], kv_[:, :, 0, :], ALU.mult)
                        V.tensor_tensor(ev[:, :, 1, :], ev[:, :, 1, :], qv_[:, :, 1, :], ALU.mult
                                        ).then_inc(level_ready, 1)
                    elif kind == "hl":
                        j, hp = s[1], s[2]
                        dst = attT[:, 2 * hp:2 * hp + 2, :, :].rearrange("p h i t -> p (h i) t")
                        msk = bc(hgmask[:, j - 1, :].unsqueeze(1), [4, P]).bitcast(U32)
                        if j > 1:
                            own((l, "hl", j - 1, hp))
                        free(V.copy_predicated(dst, msk, read(key)[:, :].rearrange("p (m t) -> p m t", m=4)), key)
                    elif kind == "ho":
                        dve.wait_ge(*bk.freed(key))
                        link(V.tensor_tensor(og2, og, og, ALU.mult))
                        V.tensor_reduce(ss8, og2, AX.X, ALU.add).then_inc(o_sums, 1)
                    elif kind == "on":
                        dve.wait_ge(o_std, l + 1)
                        link(V.reciprocal(r8, sd8))
                        link(V.tensor_tensor(og, og, bc(r8.unsqueeze(2), [8, HD]), ALU.mult))
                        link(V.tensor_tensor(og, og, bc(onorm[:, l, :].unsqueeze(1), [8, HD]), ALU.mult))
                        V.tensor_tensor(og.rearrange("p h d -> p (h d)"), og.rearrange("p h d -> p (h d)"),
                                        hgs.rearrange("p i f -> p (i f)"), ALU.mult).then_inc(og_ready, 1)
                    elif kind in ("dl", "dn"):
                        attention(dsa[l], kind, s[1])
                dve.wait_ge(gates_ready, l + 1)
                for m in range(KD):
                    y = ymul[m % 2]
                    ga = gT.rearrange("p (b m) t -> p b m t", b=3)
                    free(V.tensor_tensor(y[:, 0:512].rearrange("p (b t) -> p b t", b=2),
                                         read((l, "yab", m))[:, :].rearrange("p (b t) -> p b t", b=2),
                                         ga[:, 0:2, m, :], ALU.mult), (l, "yab", m))
                    free(V.tensor_tensor(y[:, 512:768], read((l, "yh", m))[:, 0:T], ga[:, 2, m, :], ALU.mult),
                         (l, "yh", m))
                    own((l, "yab", m))
                    link(V.tensor_tensor(y[:, 0:T], y[:, 0:T], y[:, T:2 * T], ALU.add))
                    own((l, "yh", m))
                    V.tensor_tensor(mixT[:, m, :], y[:, 0:T], y[:, 512:768], ALU.add).then_inc(mix_ready, 1)
                for n in range(2):
                    for i in range(NT):
                        xs = x[:, i, 512 * n:512 * n + 512]
                        free(V.tensor_tensor(xs, read((l, "wo", n, i))[:, :], xs, ALU.add), (l, "wo", n, i))
                norm(2 * l + 1)
                for f in range(NF):
                    dve.wait_ge(*bk.freed((l, "up", f)))
                    V.tensor_tensor(hid[:, f, :], hrl[f % 4], hrl[f % 4], ALU.mult).then_inc(hid_ready, 1)
                for n in range(2):
                    for i in range(NT):
                        xs = x[:, i, 512 * n:512 * n + 512]
                        free(V.tensor_tensor(xs, read((l, "down", n, i))[:, :], xs, ALU.add), (l, "down", n, i))

            dve.wait_ge(t5_loaded, 48)
            for g in range(DIL_G):
                key, cs = (2, "t5", g), slice(512 * g, 512 * g + 512)
                t = V.tensor_tensor(t5_rows[:, cs], read(key)[0:4, :], t5_mask[:, cs], ALU.add)
                free(t, key)
                own(key)
                V.tensor_copy(t5_rows[:, cs], t5_rows[:, cs]).then_inc(t5_masked, 1)
            norm(4)
            norm(5)

            def seg_sum(j):
                buf, col, nh, g, sc, c = segments[j]
                w = nh * HD
                dve.wait_ge(seg_squared, j + 1)
                src = squares[:, 0:NT * w].rearrange("p (i h d) -> p i h d", i=NT, h=nh)
                V.tensor_reduce(seg_ss[:, :, 0:nh], src, AX.X, ALU.add).then_inc(seg_sums, 1)

            def seg_norm(j):
                buf, col, nh, g, sc, c = segments[j]
                dve.wait_ge(seg_std, j + 1)
                link(V.reciprocal(seg_r[:, :, 0:nh], seg_sd[:, :, 0:nh]))
                if sc != 1.0:
                    link(V.tensor_scalar(seg_r[:, :, 0:nh], seg_r[:, :, 0:nh], sc, None, ALU.mult))
                v = buf[:, :, col:col + nh * HD].rearrange("p i (h d) -> p i h d", h=nh)
                for i in range(NT):
                    t = V.tensor_tensor(v[:, i], v[:, i], bc(seg_r[:, i, 0:nh].unsqueeze(2), [nh, HD]), ALU.mult)
                link(t)
                for i in range(NT):
                    t = V.tensor_tensor(v[:, i], v[:, i], bc(qkg[:, g, :].unsqueeze(1), [nh, HD]), ALU.mult)
                t.then_inc(seg_normed, 1)

            seg_sum(0)
            seg_norm(0)
            dve.wait_ge(bias_loaded, BIASES)
            nb = na_bias.rearrange("p h m c -> p (h m) c")
            link(V.tensor_tensor(nb, nb, bc(nawin.unsqueeze(1), [6 * NA_HEADS, GRID]), ALU.add))
            link(V.memset(zero_bias, 0.0))
            for c in range(8):
                if c % 2 == 1:
                    for i in range(NT):
                        free(V.tensor_copy(PP[:, i, 512 * c:512 * c + 512], read((2, "p", c, i))[:, :]), (2, "p", c, i))
                for j in range(1, len(segments)):
                    if segments[j][5] == c:
                        seg_sum(j)
                        seg_norm(j)
            for c in range(1, 24, 2):
                free(V.tensor_copy(PT[:, c, :], read((2, "pt", c))[:, 0:T]), (2, "pt", c))
            for kind, u in ATT2_STEPS:
                attention(att2, kind, u)
            for n in range(2):
                for i in range(NT):
                    xs = x[:, i, 512 * n:512 * n + 512]
                    free(V.tensor_tensor(xs, read((2, "wo", n, i))[:, :], xs, ALU.add), (2, "wo", n, i))
            norm(6)
            for i in range(NT):
                free(V.tensor_tensor(rl[:, i, :], read((2, "router", i))[:, 0:36], rbias, ALU.add), (2, "router", i))
            own((2, "router", 0))
            own((2, "router", 1))
            gl, fl = rl[:, :, 0:N_GRP], rl[:, :, N_GRP:36]
            gd, fd = bc(desc[:, N_EXP - N_GRP:].unsqueeze(1), [NT, N_GRP]), bc(desc.unsqueeze(1), [NT, N_EXP])

            def top(out_, vals, down, n, mxv, tmp):
                link(V.tensor_reduce(mxv, vals, AX.X, ALU.max))
                link(V.tensor_tensor(tmp, vals, bc(mxv, [NT, n]), ALU.is_equal))
                link(V.tensor_tensor(tmp, tmp, down, ALU.mult))
                link(V.tensor_reduce(one[11], tmp, AX.X, ALU.max))
                link(V.tensor_tensor(out_, tmp, bc(one[11], [NT, n]), ALU.is_equal))

            top(grp[0], gl, gd, N_GRP, one[0], grp[2])
            link(V.tensor_tensor(grp[1], gl, bc(one[0], [NT, N_GRP]), ALU.subtract))
            link(V.tensor_scalar(grp[3], grp[0], -1.0, -NEG, ALU.add, ALU.mult))
            for i in range(NT):
                t = V.tensor_tensor(fine[0][:, i, :].rearrange("p (g e) -> p g e", g=N_GRP),
                                    fl[:, i, :].rearrange("p (g e) -> p g e", g=N_GRP),
                                    bc(grp[3][:, i, :].unsqueeze(2), [N_GRP, EPG]), ALU.add)
            link(t)
            top(fine[1], fine[0], fd, N_EXP, one[1], fine[4])
            link(V.tensor_scalar(fine[2], fine[1], NEG * 10, None, ALU.mult))
            link(V.tensor_tensor(fine[2], fine[2], fine[0], ALU.add))
            top(fine[3], fine[2], fd, N_EXP, one[2], fine[4])
            V.tensor_tensor(one[4], one[2], one[1], ALU.subtract).then_inc(router_shifted, 1)
            dve.wait_ge(router_exps, 1)
            link(V.tensor_reduce(one[5], grp[1], AX.X, ALU.add))
            link(V.tensor_scalar(one[6], one[4], 1.0, None, ALU.add))
            link(V.tensor_tensor(one[5], one[5], one[6], ALU.mult))
            link(V.reciprocal(one[7], one[5]))
            link(V.tensor_tensor(one[8], one[7], one[4], ALU.mult))
            link(V.tensor_tensor(fine[1], fine[1], bc(one[7], [NT, N_EXP]), ALU.mult))
            link(V.tensor_tensor(fine[3], fine[3], bc(one[8], [NT, N_EXP]), ALU.mult))
            V.tensor_tensor(fine[5], fine[1], fine[3], ALU.add).then_inc(gates_made, 1)
            t = V.tensor_copy(gateT[0:N_EXP, :], read((2, "gateT"))[0:N_EXP, 0:T])
            free(t, (2, "gateT"))
            own((2, "gateT"))
            V.tensor_copy(gateT[N_EXP:N_EXP + 1, 0:8], gateT[0:1, 0:8]).then_inc(gateT_ready, 1)
            V.memset(zeros, 0.0).then_inc(zeros_set, 1)
            with dve.Fori(0, N_EXP // 2) as it:
                for e in range(2):
                    dve.wait_ge(gate_row[e], it * 16 + 16)
                    dve.wait_ge(y_step, it * 2 + (e + 1))
                    for m in range(4):
                        g = 4 * e + m
                        a_, b_ = psum[m][:, 0:T], psum[m][:, T:2 * T]
                        dve.wait_ge(sig2_ready, it * 8 + (g + 1))
                        V.tensor_tensor(hm[2 * (m % 2)], a_, sgm[m % 2], ALU.mult).then_inc(dve_step, 1)
                        dve.wait_ge(dve_step, it * 8 + (steps[0] + g + 1))
                        V.tensor_tensor(hm[2 * (m % 2) + 1], b_, hm[2 * (m % 2)], ALU.mult).then_inc(bank_free[m], 1)
                        dve.wait_ge(bank_free[m], it * 2 + (base[m] + e + 1))
                        V.tensor_tensor(aT[e][:, m, :], hm[2 * (m % 2) + 1], gate[e], ALU.mult).then_inc(aT_ready, 1)
            dve.wait_ge(y_step, N_EXP + 3)
            for i in range(NT):
                for n in range(2):
                    V.tensor_copy(x[:, i, 512 * n:512 * n + 512], psum[4 + 2 * i + n][:, :]).then_inc(out_ready, 1)


def host_constants():
    p, j = np.arange(P)[:, None], np.arange(P)[None, :]
    f = np.float32
    past = (p < j).astype(f)
    cols = [np.eye(P, dtype=f), -(p >= j).astype(f), -np.ones((P, P), f)]
    sbmask = np.concatenate([past, np.ones((P, P), f), past], axis=1)
    cols += [sbmask, (sbmask - 1) * f(1e30)]
    t = np.arange(T)[None, :]
    cols += [(t <= p + P * i).astype(f) for i in range(NT)]
    for lev in range(1, 8):
        h = HG_CHUNK >> (lev - 1)
        cols.append(((p // (2 * h) == j // (2 * h)) & (p % (2 * h) < h) & (j % (2 * h) >= h)).astype(f))
    cols.append(np.eye(P, dtype=f))
    cols.append(np.broadcast_to((t % HG_CHUNK != 0).astype(f), (P, T)))
    inv = f(500000.0) ** (-(np.arange(8, dtype=f) * f(2.0)) / f(16))
    ang = np.arange(T, dtype=f)[:, None] * inv[None, :].astype(f)
    for fn in (np.cos, np.sin):
        cols += [fn(ang[i * P:(i + 1) * P]).astype(f) for i in range(NT)]
    c, k = (np.arange(P) % GRID)[:, None], np.arange(GRID)[None, :]
    c0 = np.clip(c - 8, 0, GRID - 16)
    cols.append(np.where((k >= c0) & (k < c0 + 16), 0, NEG).astype(f))
    cols.append(np.broadcast_to((N_EXP - np.arange(N_EXP)).astype(f), (P, N_EXP)))
    main = np.ascontiguousarray(np.concatenate(cols, axis=1))
    delta = np.arange(512) - (T - 1)
    n = np.abs(delta)
    large = 8 + (np.log(np.maximum(n, 1).astype(f) / f(8)) / f(math.log(1024 / 8)) * f(8)).astype(np.int32)
    bucket = (delta > 0) * 16 + np.where(n < 8, n, np.minimum(large, 15))
    onehot, mask = np.zeros((32, 3, 512), f), np.zeros((4, 3, 512), f)
    for g, (win, dil) in enumerate(DIL):
        ok = (delta % dil == 0) & (n <= win // 2)
        onehot[bucket[ok], g, np.nonzero(ok)[0]] = 1
        mask[:, g, ~ok] = NEG
    return {"c_main": main, "c_t5": onehot.reshape(32, -1), "c_t5m": mask.reshape(4, -1)}


_INS = ['x', 'norm_mix', 'w_in', 'qn_dsa', 'kn_dsa', 'hgrn_lb', 'hgrn_onorm', 'w_br_sb', 'w_br_dsa', 'w_br_hgrn',
        'w_out', 'norm_mlp', 'w_up', 'w_down', 'mem_2', 'g_mix_2', 'w_in_2', 'qk_gain_2', 'na_rpb_2', 't5_table_2',
        'g_mem_2', 'w_mem_kv_2', 'w_out_2', 'g_ffn_2', 'w_r1_2', 'b_r1_2', 'w_r2_2', 'b_r2_2', 'w1_2', 'w3_2', 'w2_2']


def kernel(**inputs):
    import concourse.bacc as bacc
    from concourse.bass_utils import run_bass_kernel_spmd

    nc = bacc.Bacc("TRN2", target_bir_lowering=False, num_devices=1)
    arrays, aps = {}, {}
    for name, value in list((n, inputs[n]) for n in _INS) + list(host_constants().items()):
        arrays[f"in_{name}"] = np.ascontiguousarray(value)
        aps[name] = nc.dram_tensor(f"in_{name}", value.shape, F32, kind="ExternalInput").ap()
    out = nc.dram_tensor("out_0", [1, T, D], F32, kind="ExternalOutput").ap()
    build(nc, aps, out)
    result = run_bass_kernel_spmd(nc, [arrays], core_ids=[0])
    return result.results[0]["out_0"]
```

```python
import math
from contextlib import ExitStack

import numpy as np

import concourse.bass as bass
from concourse import mybir

F32 = mybir.dt.float32
U32 = mybir.dt.uint32
ALU = mybir.AluOpType
ACT = mybir.ActivationFunctionType
AX = mybir.AxisListType

P = 128
T = 256
NT = T // P
D = 1024
KD = D // P
DEPTH = 2
HD = 64
EPS = 1e-6
F_MIN = 1e-12
NEG = -1e30

N_SB, N_DSA, N_IDX, N_HG, HG_DV, HG_CHUNK = 6, 6, 8, 4, 64, 64
SPLITS = [("sq", 384), ("sk", 384), ("sv", 384), ("dq", 384), ("dk", 64), ("dv", 64), ("iq", 512),
          ("ik", 64), ("iw", 8), ("hq", 512), ("hf", 512), ("hi", 256), ("hg", 256),
          ("gsb", 1024), ("gdsa", 1024), ("ghg", 1024)]
COL = {}
_at = 0
for _n, _w in SPLITS:
    COL[_n] = _at
    _at += _w
D_IN = _at
IDX_SCALE = float((64 * N_IDX) ** -0.5)
TOPK = 64
RH = 18
D_FF = 4 * D
NF = D_FF // P

NA_HEADS, DIL_HPG, DIL_G, MEM_HEADS = 8, 4, 3, 4
IN2 = 4096
GRID = 64
N_EXP, N_GRP, EPG = 32, 4, 8
D_EXP = 512
DIL = ((128, 1), (512, 4), (2048, 16))

SLOTS = 4
CAP = 64
MSLOTS = 6
RING = 6


def chunks_of_layer(l):
    c = [("w_in", 0, 8, COL["sq"], 384), ("w_in", 0, 8, COL["sk"], 384), ("w_in", 0, 8, COL["sv"], 384),
         ("w_in", 0, 8, COL["dq"], 512), ("w_in", 0, 8, COL["iq"], 512), ("w_in", 0, 8, COL["ik"], 72),
         ("w_in", 0, 8, COL["hq"], 512), ("w_in", 0, 8, COL["hf"], 512), ("w_in", 0, 8, COL["hi"], 256),
         ("w_in", 0, 8, COL["hg"], 256)]
    c += [("w_in", 0, 8, COL["gsb"] + 512 * j, 512) for j in range(6)]
    c += [("w_br", 0, 8, 512 * j, 512) for j in range(2)]
    c += [("w_out", 0, 8, 512 * j, 512) for j in range(2)]
    c += [("w_up", 0, 8, 512 * j, 512) for j in range(8)]
    c += [("w_down", 1024 * kb, 8, 512 * n, 512) for kb in range(4) for n in range(2)]
    return [(l,) + x for x in c]


def chunks_of_block2():
    c = [("w_mem_kv_2", 0, 8, 0, 512)]
    c += [("w_in_2", 0, 8, 512 * j, 512) for j in range(8)]
    c += [("w_out_2", 0, 8, 512 * j, 512) for j in range(2)]
    return [(0,) + x for x in c]


def mixer_steps():
    s = [("rt", c) for c in range(9)]
    for h in range(N_SB + 2):
        if h < N_SB:
            s.append(("z", h))
        if 1 <= h <= N_SB:
            s.append(("u", h - 1))
        if h >= 3 and h % 2 == 1:
            s.append(("o", (h - 3) // 2))
    s.append(("hp", 0))
    for i in range(NT):
        s += [("ix", i, j) for j in range(N_IDX)]
        s.append(("tk", i))
    s += [("lv", 0), ("lv", 1)]
    for j in range(9):
        if j <= 7:
            s.append(("lm", j))
        s += [("hx",)] if j == 0 else [("hl", j, 0), ("hl", j, 1)]
        if j + 2 <= 7:
            s.append(("lv", j + 2))
    s.append(("ho",))
    n = N_DSA * NT
    for u in range(n + 3):
        for kind, v in (("dl", u), ("dn", u - 1), ("dt", u - 2), ("dp", u - 3)):
            if 0 <= v < n:
                s.append((kind, v))
    s += [("on",), ("oht", 0), ("oht", 1)]
    weights = {"rt": 0.1, "z": 0.7, "u": 0.7, "o": 0.7, "hp": 2.0, "ix": 0.3, "tk": 3.0, "lv": 1.5, "lm": 1.5,
               "hl": 0.7, "hx": 0.7, "ho": 1.0, "dl": 0.2, "dn": 0.2, "dt": 0.2, "dp": 0.2, "on": 0.5, "oht": 0.5}
    total = sum(weights[x[0]] for x in s)
    out, g, past = [], 0, 0.0
    for x in s:
        while g < 24 and g * total <= past * 24:
            out.append(("g", g))
            g += 1
        out.append(x)
        past += weights[x[0]]
    out += [("g", g) for g in range(g, 24)]
    return out


MIX = mixer_steps()


def attn_steps(n):
    s = []
    for u in range(n + 3):
        for kind, v in (("dl", u), ("dn", u - 1), ("dt", u - 2), ("dp", u - 3)):
            if 0 <= v < n:
                s.append((kind, v))
    return s


class Banks:

    def __init__(self, full, free):
        self.full_sem, self.free_sem = full, free
        self.uses = [0] * 8
        self.turn, self.long_turn = 0, 0
        self.at = {}

    def give(self, key, long=False):
        if long:
            b = RING + self.long_turn % 2
            self.long_turn += 1
        else:
            b = self.turn % RING
            self.turn += 1
        assert key not in self.at, key
        self.at[key] = (b, self.uses[b])
        self.uses[b] += 1

    def bank(self, key):
        return self.at[key][0]

    def full(self, key):
        b, u = self.at[key]
        return self.full_sem[b], u + 1

    def freed(self, key):
        b, u = self.at[key]
        return self.free_sem[b], u + 1

    def before(self, key):
        b, u = self.at[key]
        return self.free_sem[b], u


def build(nc, a, out):
    ctx = ExitStack()
    with ctx:
        ctx.enter_context(nc.allow_non_contiguous_dma(reason="parameter columns of a few KiB"))

        def sb(name, shape, dt=F32):
            return ctx.enter_context(nc.sbuf_tensor(name, shape, dt))

        def sem(name):
            return ctx.enter_context(nc.semaphore(name))

        CW = a["c_main"].shape[1]
        ring = sb("ring", [P, SLOTS, KD, 512])
        cst = sb("cst", [P, CW])
        x = sb("x", [P, NT, D])
        hT = sb("hT", [P, KD, T])
        par = sb("par", [P, 1160])
        small = sb("small", [P, 512])
        REGION = 27584
        region = sb("region", [P, REGION])

        class Cutter:

            def __init__(self, tile, end, at=0):
                self.tile, self.end, self.at = tile, end, at

            def cut(self, *dims):
                n = math.prod(dims)
                v = self.tile[:, self.at:self.at + n]
                self.at += n
                assert self.at <= self.end, self.at
                if len(dims) == 2:
                    v = v.rearrange("p (a b) -> p a b", a=dims[0])
                elif len(dims) == 3:
                    v = v.rearrange("p (a b c) -> p a b c", a=dims[0], b=dims[1])
                return v

        c_ = Cutter(cst, CW).cut
        ident, negtri, negones = c_(P), c_(P), c_(P)
        sbmask, sbneg = c_(384), c_(384)
        causal = c_(NT, T)
        hgmask = c_(8, P)
        scan0 = c_(T)
        cosT, sinT = c_(NT, 8), c_(NT, 8)
        nawin = c_(GRID)
        desc = c_(N_EXP)
        slot_no = c_(64)
        p_ = Cutter(par, 1160).cut
        g_mix, g_mlp = p_(DEPTH, KD), p_(DEPTH, KD)
        g_mix2, g_mem2, g_ffn2 = p_(KD), p_(KD), p_(KD)
        lbraw = p_(DEPTH, N_HG)
        qn, kn, onorm = p_(DEPTH, HD), p_(DEPTH, HD), p_(DEPTH, HD)
        qkg = p_(6, HD)
        rbias = p_(36)
        wr = p_(KD, 36)
        s_ = Cutter(small, 512).cut
        eps_c = s_(1)
        ss, sd, rstd = s_(2), s_(2), s_(2)
        lb, omlb = s_(DEPTH, N_HG), s_(DEPTH, N_HG)
        lb_m, lb_s, lb_r = s_(N_HG), s_(N_HG), s_(N_HG)
        lb_e = s_(DEPTH, N_HG)
        ss14, sd14, r14 = s_(NT, 7), s_(NT, 7), s_(NT, 7)
        ss8, sd8, r8 = s_(8), s_(8), s_(8)
        iw = s_(NT, N_IDX)
        top8 = s_(8)
        mx = s_(4, 3)
        nmax, esum, rsum = s_(4), s_(4), s_(4)
        seg_ss, seg_sd, seg_r = s_(NT, 12), s_(NT, 12), s_(NT, 12)

        A = Cutter(region, REGION)
        sqT, skT, sv = A.cut(3, T), A.cut(3, T), A.cut(NT, 384)
        E = [Cutter(region, REGION, 1024 * j).cut(N_HG, T) for j in range(2)]
        dv = A.cut(NT, HD)
        at_RT = A.at
        RT = A.cut(9, T)
        ymul = [Cutter(region, REGION, at_RT + 768 * j).cut(768) for j in range(2)]
        at_R = A.at
        R = A.cut(NT, RH, HD)
        mixT = Cutter(region, REGION, at_R).cut(KD, T)
        hqT = A.cut(N_HG, T)
        at_f = A.at
        fT = A.cut(N_HG, T)
        og, og2 = Cutter(region, REGION, at_f).cut(8, HD), Cutter(region, REGION, at_f + 512).cut(8, HD)
        kT, bT = A.cut(N_HG, T), A.cut(N_HG, T)
        attT, attX = A.cut(N_HG, NT, P), A.cut(N_HG, P)
        hv, hgs = A.cut(NT, T), A.cut(NT, T)
        sbL = [A.cut(384) for _ in range(2)]
        sbA = [A.cut(384) for _ in range(4)]
        at_rel = A.at
        rel = [A.cut(T) for _ in range(2)]
        score, negsel = A.cut(NT, T), A.cut(NT, T)
        osT, odT, ohT = A.cut(3, T), A.cut(3, T), A.cut(2, T)
        prb = [A.cut(T) for _ in range(4)]
        prT = [A.cut(NT, P) for _ in range(3)]
        hsg = [Cutter(region, REGION, at_f + 1024 + 256 * j).cut(T) for j in range(2)]
        gT = A.cut(24, T)
        xn = gT[:, 0:8, :].rearrange("p m t -> p (m t)").rearrange("p (i d) -> p i d", i=NT)
        ra = Cutter(region, REGION, at_rel).cut(896)
        sq14 = ra.rearrange("p (i h d) -> p i h d", i=NT, h=7)
        M = Cutter(region, REGION)
        hid = M.cut(NF, T)
        hrl = [M.cut(T) for _ in range(4)]

        C = Cutter(region, REGION)
        xn2, memT = C.cut(NT, D), C.cut(KD, T)
        PP, kv = C.cut(NT, IN2), C.cut(NT, 512)
        PT = C.cut(24, T)
        na_bias = C.cut(NA_HEADS, 6, GRID)
        dil_bias = C.cut(12, 384)
        xn2_flat = xn2.rearrange("p i d -> p (i d)")
        memT_flat = memT.rearrange("p k t -> p (k t)")
        PT_flat = PT.rearrange("p c t -> p (c t)")
        hT_flat = hT[:, :, :].rearrange("p k t -> p (k t)")
        prb2 = [hT_flat[:, 0:768], hT_flat[:, 768:1536], xn2_flat[:, 0:768], xn2_flat[:, 768:1536]]
        prT2 = [memT_flat[:, 0:768].rearrange("p (s t) -> p s t", s=6),
                memT_flat[:, 768:1536].rearrange("p (s t) -> p s t", s=6),
                PP[:, 0, 2304:3072].rearrange("p (s t) -> p s t", s=6)]
        zero_bias = memT_flat[:, 1536:1792]
        squares = xn2_flat[:, 0:1536]
        t5_onehot, t5_tab = PT_flat[0:32, 0:1536], PT_flat[0:32, 1536:1548]
        t5_mask, t5_rows = PT_flat[0:4, 2048:3584], PT_flat[0:4, 4096:5632]

        def oT2(c):
            return PP[:, c // 4, T * (c % 4):T * (c % 4) + T]

        X = Cutter(region, REGION)
        wslot = [ring[:, j, :, :] for j in range(SLOTS)] + [X.cut(KD, 512) for _ in range(MSLOTS - SLOTS)]
        xn3 = X.cut(NT, D)
        rl = X.cut(NT, 36)
        grp = [X.cut(NT, N_GRP) for _ in range(6)]
        fine = [X.cut(NT, N_EXP) for _ in range(6)]
        one = [X.cut(NT, 1) for _ in range(12)]
        gateT = X.cut(T)
        zeros = X.cut(P)
        gain_row = X.cut(D)
        at_pick = X.at
        pick = X.cut(NT, N_EXP, 64)
        put = X.cut(N_EXP // 2, T)
        at_put0 = X.at
        put0 = X.cut(NT, N_EXP, 64)
        S = Cutter(region, REGION, at_put0)
        xg, yslot = S.cut(KD, P), S.cut(D)
        pair_hid, hms = S.cut(512), S.cut(512)
        aTs = [S.cut(4, 64) for _ in range(2)]
        S = Cutter(region, REGION, at_pick)
        yT = S.cut(KD, T)
        S = Cutter(region, REGION, at_pick)
        aT = [S.cut(4, T) for _ in range(2)]
        gate = [S.cut(T) for _ in range(2)]
        sgm = [S.cut(T) for _ in range(2)]
        hm = [S.cut(T) for _ in range(4)]
        overflow = sb("overflow", [1, 8], mybir.dt.int32)

        psum = [ctx.enter_context(nc.psum_tensor(f"bank{b}", [P, 512], F32)) for b in range(8)]

        NA_ROW = NA_HEADS * 15 * 31
        na_dram = nc.dram_tensor("na_bias_rows", [GRID, NA_ROW], F32, kind="Internal").ap()
        t5_dram = nc.dram_tensor("t5_bias_rows", [12, P, 512], F32, kind="Internal").ap()
        gate_dram = nc.dram_tensor("gate_rows", [N_EXP, T], F32, kind="Internal").ap()

        bank_full = [sem(f"bank{b}_full") for b in range(8)]
        bank_free = [sem(f"bank{b}_free") for b in range(8)]
        slot_full = [sem(f"slot{j}_full") for j in range(MSLOTS)]
        (down_chunk_used, consts_loaded, x_loaded, params_loaded, eps_set, act_step, dve_step, std_ready,
         rows_normed, log1p_ready, sp_ready, sba_ready, head_sums, head_std, R_ready, sig_ready, f_ready,
         logf_ready, level_exponents, level_exps, level_ready, o_sums, o_std, og_ready, rel_used, rowmax_ready,
         exps_ready, probs_ready, probsT_used, gates_ready, mix_ready, hid_ready, lb_shifted, lb_exps,
         mem_loaded, t5_loaded, t5_masked, t5_stored, bias_loaded, seg_squared, seg_sums, seg_std, seg_normed,
         router_shifted, router_exps, gates_made, gateT_ready, gate_stored, y_step, aT_ready, sig2_ready,
         out_ready, out_stored, na_stored, zeros_set, gain0_loaded, gain_row_loaded, picks_made, pick_ready, put0_ready, h_rows_ready, overflow_known, experts_up, dense_step, sums_done) = [sem(n) for n in (
             "down_chunk_used consts_loaded x_loaded params_loaded eps_set act_step dve_step std_ready "
             "rows_normed log1p_ready sp_ready sba_ready head_sums head_std R_ready sig_ready f_ready "
             "logf_ready level_exponents level_exps level_ready o_sums o_std og_ready rel_used rowmax_ready "
             "exps_ready probs_ready probsT_used gates_ready mix_ready hid_ready lb_shifted lb_exps "
             "mem_loaded t5_loaded t5_masked t5_stored bias_loaded seg_squared seg_sums seg_std seg_normed "
             "router_shifted router_exps gates_made gateT_ready gate_stored y_step aT_ready sig2_ready "
             "out_ready out_stored na_stored zeros_set gain0_loaded "
             "gain_row_loaded picks_made pick_ready put0_ready h_rows_ready overflow_known experts_up dense_step sums_done").split()]
        gate_row = [sem(f"gate_row{j}") for j in range(2)]

        chunks = chunks_of_layer(0) + chunks_of_layer(1) + chunks_of_block2()
        CL, NCH = len(chunks_of_layer(0)), len(chunks)
        arrive, slot_total = [], [0] * MSLOTS
        for n, c in enumerate(chunks):
            slot_total[n % SLOTS] += 16 * (3 if c[1] == "w_br" else 1)
            arrive.append((slot_full[n % SLOTS], slot_total[n % SLOTS]))

        def slot(n):
            return ring[:, n % SLOTS, :, :]

        bk = Banks(bank_full, bank_free)
        last_use = [None] * NCH
        for l in range(DEPTH):
            c0 = l * CL
            for k in range(KD):
                bk.give((l, "hT", k))
            for n, w in (("sq", 3), ("sk", 3), ("sv", 2), ("d", 2), ("iq", 2), ("ik", 2), ("hq", 4),
                         ("hf", 4), ("hi", 2), ("hg", 2)):
                for m in range(w):
                    bk.give((l, n, m))
                last_use[c0] = bk.full((l, n, w - 1))
                c0 += 1
            for s in MIX:
                if s[0] in ("g", "rt", "z", "u", "o", "ix", "hl", "hx", "ho", "oht"):
                    bk.give((l,) + s)
                    if s[0] == "g" and s[1] % 4 == 3:
                        last_use[c0] = bk.full((l,) + s)
                        c0 += 1
                elif s[0] in ("dl", "dt"):
                    bk.give((l, s[0], s[1], 0))
                elif s[0] == "dp" and s[1] % 4 == 0:
                    bk.give((l, "pair", s[1] // 4), long=True)
            for m in range(KD):
                bk.give((l, "yab", m))
                bk.give((l, "yh", m))
                if m % 4 == 3:
                    last_use[c0] = bk.full((l, "yh", m))
                    c0 += 1
            for n in range(2):
                for i in range(NT):
                    bk.give((l, "wo", n, i))
                last_use[c0] = bk.full((l, "wo", n, 1))
                c0 += 1
            for k in range(KD):
                bk.give((l, "h2T", k))
            for f in range(NF):
                bk.give((l, "up", f))
                if f % 4 == 3:
                    last_use[c0] = bk.full((l, "up", f))
                    c0 += 1
            for n in range(2):
                for i in range(NT):
                    bk.give((l, "down", n, i))
            for c in range(6):
                last_use[c0] = (down_chunk_used, 6 * l + c + 1)
                c0 += 1
            for n in range(2):
                last_use[c0] = bk.full((l, "down", n, 1))
                c0 += 1
            assert c0 == (l + 1) * CL

        class Attention:

            def __init__(self, tag, first, units, prb, prT, pair_out):
                self.tag, self.first, self.units = tag, first, units
                self.prb, self.prT, self.pair_out = prb, prT, pair_out

        dsa, upl = [], N_DSA * NT
        for l in range(DEPTH):
            units = []
            for u in range(upl):
                pair, i, hh = u // 4, (u // 2) % 2, u % 2
                units.append(([(RT[:, pair, :], RT[:, 3, :], negsel[:, i, :], [dv[:, kt, :] for kt in range(NT)])],
                              i, 64 * hh))
            dsa.append(Attention(l, l * upl, units, prb, prT, lambda pair: odT[:, pair, :]))
        units2 = []
        for pair in range(KD):
            for i in range(NT):
                for hh in range(2):
                    if pair < 4:
                        h, m0 = 2 * pair + hh, 2 - 2 * i
                        segs = [(PT[:, pair, :], PT[:, 4 + pair, :],
                                 na_bias[:, h, m0:m0 + 4, :].rearrange("p m c -> p (m c)"),
                                 [PP[:, kt, 1024 + 64 * h:1088 + 64 * h] for kt in range(NT)])]
                    elif pair < 6:
                        h, c0 = 2 * (pair - 4) + hh, P - P * i
                        segs = [(PT[:, 8 + 2 * g + pair - 4, :], PT[:, 14 + 2 * g + pair - 4, :],
                                 dil_bias[:, 4 * g + h, c0:c0 + T],
                                 [PP[:, kt, 3072 + 256 * g + 64 * h:3136 + 256 * g + 64 * h] for kt in range(NT)])
                                for g in range(DIL_G)]
                    else:
                        h = 2 * (pair - 6) + hh
                        segs = [(PT[:, 14 + pair, :], PT[:, 16 + pair, :], zero_bias,
                                 [kv[:, kt, 256 + 64 * h:320 + 64 * h] for kt in range(NT)])]
                    units2.append((segs, i, 64 * hh))
        att2 = Attention(2, DEPTH * upl, units2, prb2, prT2, oT2)
        ATT2_STEPS = attn_steps(len(units2))

        c0 = DEPTH * CL
        for g in range(DIL_G):
            bk.give((2, "t5", g))
        for k in range(KD):
            bk.give((2, "memT", k))
        for i in range(NT):
            bk.give((2, "kv", i))
        last_use[c0] = bk.full((2, "kv", 1))
        for k in range(KD):
            bk.give((2, "hT", k))
        for c in range(8):
            for i in range(NT):
                bk.give((2, "p", c, i))
            last_use[c0 + 1 + c] = bk.full((2, "p", c, 1))
        for c in range(24):
            bk.give((2, "pt", c))
        for s in ATT2_STEPS:
            if s[0] in ("dl", "dt"):
                for g in range(len(units2[s[1]][0])):
                    bk.give((2, s[0], s[1], g))
            elif s[0] == "dp" and s[1] % 4 == 0:
                bk.give((2, "pair", s[1] // 4), long=True)
        for n in range(2):
            for i in range(NT):
                bk.give((2, "wo", n, i))
            last_use[c0 + 9 + n] = bk.full((2, "wo", n, 1))
        for k in range(KD):
            bk.give((2, "h2T", k))
        for i in range(NT):
            bk.give((2, "router", i))
        bk.give((2, "rank"))
        bk.give((2, "gateT"))
        for j in range(8):
            bk.give((2, "put", j))
        base = list(bk.uses)
        ROUNDS = N_EXP // 2
        base2 = [base[b] + ROUNDS * (3, 2, 3, 2, 0, 0, 0, 0)[b] + 1 for b in range(8)]

        segments = [(kv, 0, 4, 5, 1.0, 0), (PP, 0, 8, 0, 0.125, 0), (PP, 512, 8, 1, 1.0, 1),
                    (PP, 1536, 12, 2, 0.125, 4), (PP, 2304, 12, 3, 1.0, 5), (PP, 3840, 4, 4, 0.125, 7)]
        tiles2 = [(PP, 128 * c) for c in range(8)] + [(PP, 1536 + 128 * c) for c in range(12)] + \
                 [(PP, 3840), (PP, 3968), (kv, 0), (kv, 128)]

        wo_done = [[bk.freed((l, "wo", n, i)) for n in range(2) for i in range(NT)] for l in range(3)]
        down_done = [[bk.freed((l, "down", n, i)) for n in range(2) for i in range(NT)] for l in range(DEPTH)]
        norms = [(x, [(x_loaded, 16)], xn, (0, "hT"), g_mix[:, 0, :], hT),
                 (x, wo_done[0], xn, (0, "h2T"), g_mlp[:, 0, :], hT),
                 (x, down_done[0], xn, (1, "hT"), g_mix[:, 1, :], hT),
                 (x, wo_done[1], xn, (1, "h2T"), g_mlp[:, 1, :], hT),
                 (xn2, [(mem_loaded, 16)], xn2, (2, "memT"), g_mem2, memT),
                 (x, down_done[1], xn2, (2, "hT"), g_mix2, hT),
                 (x, wo_done[2], xn3, (2, "h2T"), g_ffn2, hT)]

        def load_expert(queue, q, ex):
            src = a[("w1_2", "w3_2", "w2_2")[q % 3]][0, bass.ds(ex, 1), :, :].rearrange("e (k p) n -> p (e k) n", p=P)
            dst = wslot[q]
            if q % 3 == 2:
                dst = dst.rearrange("p k n -> p (k n)").rearrange("p (k n) -> p k n", k=4)
            queue.dma_start(dst, src).then_inc(slot_full[q], 16)

        block = ctx.enter_context(nc.Block())

        @block.sync
        def _(sp):
            sp.dma_start(x[:, :, :], a["x"].rearrange("b (i p) d -> p (b i) d", p=P)).then_inc(x_loaded, 16)
            sp.dma_start(cst[:, :], a["c_main"]).then_inc(consts_loaded, 16)
            for n, (l, name, r0, kt, c0, w) in enumerate(chunks):
                if n >= SLOTS:
                    sp.wait_ge(*last_use[n - SLOTS])
                s = slot(n)
                if name == "w_br":
                    k = 0
                    for part, kk in (("w_br_sb", 3), ("w_br_dsa", 3), ("w_br_hgrn", 2)):
                        src = a[part][l, :, c0:c0 + w].rearrange("(k p) n -> p k n", p=P)
                        sp.dma_start(s[:, k:k + kk, 0:w], src).then_inc(arrive[n][0], 16)
                        k += kk
                else:
                    src = a[name][l, r0:r0 + kt * P, c0:c0 + w].rearrange("(k p) n -> p k n", p=P)
                    sp.dma_start(s[:, 0:kt, 0:w], src).then_inc(arrive[n][0], 16)
            for n in range(NCH - SLOTS, NCH):
                sp.wait_ge(*last_use[n])
            for w in wo_done[2]:
                sp.wait_ge(*w)

            with sp.Fori(0, ROUNDS) as it:
                sp.wait_ge(bank_full[2], it * 3 + (base[2] - 2))
                load_expert(sp, 0, it * 2)
                sp.wait_ge(bank_full[2], it * 3 + (base[2] - 1))
                load_expert(sp, 3, it * 2 + 1)
                sp.wait_ge(y_step, it + 1)
                load_expert(sp, 2, it * 2)
            sp.wait_ge(overflow_known, 1)
            more = sp.value_load(overflow[0:1, 0:1], min_val=0, max_val=1)
            with sp.If(more > 0):
                sp.wait_ge(gate_stored, 16)
                with sp.Fori(0, ROUNDS) as it:
                    for e in range(2):
                        sp.wait_ge(dense_step, it * 2 + (e + 1))
                        sp.dma_start(gate[e], gate_dram[bass.ds(it * 2 + e, 1), :].broadcast_to([P, T])
                                     ).then_inc(gate_row[e], 16)
                        for q in range(3 * e, 3 * e + 3):
                            load_expert(sp, q, it * 2 + e)

        n_params = [0]

        @block.gpsimd
        def _(pool):
            def col(dst, src):
                pool.dma_start(dst, src.rearrange("(k p) -> p k", p=P)).then_inc(params_loaded, 16)
                n_params[0] += 16

            def row(dst, src, w):
                pool.dma_start(dst, src.unsqueeze(0).broadcast_to([P, w])).then_inc(params_loaded, 16)
                n_params[0] += 16

            pool.dma_start(g_mix[:, 0, :], a["norm_mix"][0].rearrange("(k p) -> p k", p=P)).then_inc(gain0_loaded, 16)
            for l in range(DEPTH):
                if l:
                    col(g_mix[:, l, :], a["norm_mix"][l])
                col(g_mlp[:, l, :], a["norm_mlp"][l])
                col(lbraw[:, l, :], a["hgrn_lb"][l])
                row(qn[:, l, :], a["qn_dsa"][l], HD)
                row(kn[:, l, :], a["kn_dsa"][l], HD)
                row(onorm[:, l, :], a["hgrn_onorm"][l], HD)
            col(g_mix2, a["g_mix_2"][0])
            col(g_mem2, a["g_mem_2"][0])
            col(g_ffn2, a["g_ffn_2"][0])
            for j in range(6):
                row(qkg[:, j, :], a["qk_gain_2"][0, j // 2, j % 2], HD)
            row(rbias[:, 0:N_GRP], a["b_r1_2"][0], N_GRP)
            row(rbias[:, N_GRP:36], a["b_r2_2"][0], N_EXP)
            for dst, name in ((wr[:, :, 0:N_GRP], "w_r1_2"), (wr[:, :, N_GRP:36], "w_r2_2")):
                pool.dma_start(dst, a[name][0].rearrange("(k p) n -> p k n", p=P)).then_inc(params_loaded, 16)
                n_params[0] += 16
            for w in down_done[DEPTH - 1]:
                pool.wait_ge(*w)
            pool.dma_start(xn2, a["mem_2"].rearrange("b (i p) d -> p (b i) d", p=P)).then_inc(mem_loaded, 16)
            pool.dma_start(t5_onehot, a["c_t5"]).then_inc(t5_loaded, 16)
            pool.dma_start(t5_mask, a["c_t5m"]).then_inc(t5_loaded, 16)
            pool.dma_start(t5_tab, a["t5_table_2"]).then_inc(t5_loaded, 16)
            rows, cols = 15, 31
            pool.dma_start(na_dram, a["na_rpb_2"].rearrange("l h r c -> l (h r c)").broadcast_to([GRID, NA_ROW])
                           ).then_inc(na_stored, 16)
            pool.wait_ge(na_stored, 16)
            for r in range(2):
                for h in range(NA_HEADS):
                    src = bass.AP(tensor=na_dram.tensor, offset=(h * rows + 5 - r) * cols + 15,
                                  ap=[[NA_ROW - 1, GRID], [cols, 6], [1, GRID]])
                    pool.dma_start(na_bias[64 * r:64 * r + 64, h, :, :], src).then_inc(bias_loaded, 16)
            pool.wait_ge(t5_masked, DIL_G)
            for g in range(DIL_G):
                pool.dma_start(t5_dram[4 * g:4 * g + 4, :, :],
                               t5_rows[:, 512 * g:512 * g + 512].unsqueeze(1).broadcast_to([4, P, 512])
                               ).then_inc(t5_stored, 16)
            pool.wait_ge(t5_stored, 16 * DIL_G)
            for h in range(12):
                src = bass.AP(tensor=t5_dram.tensor, offset=h * P * 512 + 127, ap=[[511, P], [1, 384]])
                pool.dma_start(dil_bias[:, h, :], src).then_inc(bias_loaded, 16)
            for w in wo_done[2]:
                pool.wait_ge(*w)
            pool.dma_start(gain_row, a["g_ffn_2"].broadcast_to([P, D])).then_inc(gain_row_loaded, 16)
            pool.wait_ge(gateT_ready, 1)
            pool.dma_start(gate_dram, gateT[0:N_EXP, :]).then_inc(gate_stored, 16)
            for i in range(NT):
                pool.wait_ge(out_ready, 1)
                pool.dma_start(out.rearrange("b (i p) d -> p (b i) d", p=P)[:, i, :], x[:, i, :]
                               ).then_inc(out_stored, 16)
            pool.wait_ge(out_stored, 16 * NT)

        BIASES = 16 * (2 * NA_HEADS + 12)

        @block.tensor
        def _(pe):
            mm, turn = nc.tensor.matmul, nc.tensor.transpose

            def bank_of(key):
                if bk.at[key][1]:
                    pe.wait_ge(*bk.before(key))
                return psum[bk.bank(key)]

            def full(ins, key):
                ins.then_inc(bank_full[bk.bank(key)], 1)

            def arrived(n):
                pe.wait_ge(*arrive[n])
                return slot(n)

            def wait_freed(keys):
                for k in keys:
                    pe.wait_ge(*bk.freed(k))

            def turn_rows(n):
                _, _, src, (l, name), _, _ = norms[n]
                pe.wait_ge(rows_normed, 2 * (n + 1))
                for k in range(KD):
                    b = bank_of((l, name, k))
                    for i in range(NT):
                        t = turn(b[:, i * P:(i + 1) * P], src[:, i, k * P:(k + 1) * P], ident)
                    full(t, (l, name, k))
                wait_freed([(l, name, k) for k in range(KD)])

            def feature_major(key, w, act):
                b = bank_of(key)
                for k in range(KD):
                    t = mm(b[:, 0:T], w[:, k, :], act[:, k, :], start=(k == 0), stop=(k == KD - 1))
                full(t, key)

            def token_major(key, w, act, i):
                b, cols = bank_of(key), w.shape[2]
                for k in range(KD):
                    t = mm(b[:, 0:cols], act(k)[:, i * P:(i + 1) * P], w[:, k, :],
                           start=(k == 0), stop=(k == KD - 1))
                full(t, key)

            def h_tile(k):
                return hT[:, k, :]

            def attention(at, kind, u):
                segs, i, b0 = at.units[u]
                U = at.first + u
                if kind == "dl":
                    for g, (q, kk, _, _) in enumerate(segs):
                        b = bank_of((at.tag, "dl", u, g))
                        t = mm(b[:, 0:T], q[b0:b0 + 64, i * P:(i + 1) * P], kk[b0:b0 + 64, :], start=True, stop=True)
                        full(t, (at.tag, "dl", u, g))
                elif kind == "dt":
                    pe.wait_ge(probs_ready, U + 1)
                    for g in range(len(segs)):
                        b = bank_of((at.tag, "dt", u, g))
                        for kt in range(NT):
                            c = T * g + P * kt
                            t = turn(b[:, kt * P:(kt + 1) * P], at.prb[U % 4][:, c:c + P], ident)
                        full(t, (at.tag, "dt", u, g))
                elif kind == "dp":
                    key = (at.tag, "pair", u // 4)
                    b = bank_of(key) if u % 4 == 0 else psum[bk.bank(key)]
                    wait_freed([(at.tag, "dt", u, g) for g in range(len(segs))])
                    n = 0
                    for g, (_, _, _, v) in enumerate(segs):
                        for kt in range(NT):
                            t = mm(b[b0:b0 + 64, i * P:(i + 1) * P], v[kt], at.prT[U % 3][:, NT * g + kt, :],
                                   start=(n == 0), stop=(n == NT * len(segs) - 1))
                            n += 1
                    t.then_inc(probsT_used, 1)

            pe.wait_ge(consts_loaded, 16)
            for l in range(DEPTH):
                c0 = l * CL
                turn_rows(2 * l)
                for c, name in ((0, "sq"), (1, "sk")):
                    w = arrived(c0 + c)
                    for m in range(3):
                        feature_major((l, name, m), w[:, :, P * m:P * m + P], hT)
                for c, name, cols in ((2, "sv", 384), (3, "d", 512), (4, "iq", 512), (5, "ik", 72)):
                    w = arrived(c0 + c)
                    for i in range(NT):
                        token_major((l, name, i), w[:, :, 0:cols], h_tile, i)
                for c, name in ((6, "hq"), (7, "hf")):
                    w = arrived(c0 + c)
                    for m in range(4):
                        feature_major((l, name, m), w[:, :, P * m:P * m + P], hT)
                for c, name in ((8, "hi"), (9, "hg")):
                    w = arrived(c0 + c)
                    for i in range(NT):
                        token_major((l, name, i), w[:, :, 0:T], h_tile, i)

                for s in MIX:
                    kind, key = s[0], (l,) + s
                    if kind == "g":
                        m = s[1]
                        w = arrived(c0 + 10 + m // 4)
                        feature_major(key, w[:, :, P * (m % 4):P * (m % 4) + P], hT)
                    elif kind == "rt":
                        pe.wait_ge(R_ready, l + 1)
                        b, c = bank_of(key), s[1]
                        for i in range(NT):
                            t = turn(b[:, i * P:(i + 1) * P], R[:, i, 2 * c:2 * c + 2, :].rearrange("p h d -> p (h d)"),
                                     ident)
                        full(t, key)
                    elif kind in ("z", "u"):
                        h = s[1]
                        r = slice(64 * (h % 2), 64 * (h % 2) + 64)
                        q, kk = sqT[r, h // 2, :], skT[r, h // 2, :]
                        if h == 0:
                            wait_freed([(l, n, m) for n in ("sq", "sk") for m in range(3)])
                        if kind == "z":
                            b = bank_of(key)
                            mm(b[:, 0:T], kk[:, 0:P], q, start=True, stop=True)
                            t = mm(b[:, T:T + P], kk[:, P:T], q[:, P:T], start=True, stop=True)
                        else:
                            pe.wait_ge(sp_ready, l * N_SB + h + 1)
                            b, L = bank_of(key), sbL[h % 2]
                            mm(b[:, 0:P], kk[:, 0:P], q[:, 0:P], start=True, stop=False)
                            mm(b[:, 0:P], negtri, L[:, 0:P], start=False, stop=True)
                            mm(b[:, P:T], kk[:, 0:P], q[:, P:T], start=True, stop=False)
                            mm(b[:, P:T], negtri, L[:, P:T], start=False, stop=False)
                            mm(b[:, P:T], negones, L[:, T:T + P], start=False, stop=True)
                            mm(b[:, T:T + P], kk[:, P:T], q[:, P:T], start=True, stop=False)
                            t = mm(b[:, T:T + P], negtri, L[:, T:T + P], start=False, stop=True)
                        full(t, key)
                    elif kind == "o":
                        pr = s[1]
                        if pr == 0:
                            wait_freed([(l, "sv", 0), (l, "sv", 1)])
                        pe.wait_ge(sba_ready, l * N_SB + 2 * pr + 2)
                        b = bank_of(key)
                        for hh in range(2):
                            h = 2 * pr + hh
                            w_, o_ = sbA[h % 4], b[64 * hh:64 * hh + 64, :]
                            mm(o_[:, 0:P], sv[:, 0, HD * h:HD * h + HD], w_[:, 0:P], start=True, stop=True)
                            mm(o_[:, P:T], sv[:, 0, HD * h:HD * h + HD], w_[:, P:T], start=True, stop=False)
                            t = mm(o_[:, P:T], sv[:, 1, HD * h:HD * h + HD], w_[:, T:T + P], start=False, stop=True)
                        full(t, key)
                    elif kind == "ix":
                        i, j = s[1], s[2]
                        if i == 0 and j == 0:
                            wait_freed([(l, "rt", c) for c in range(9)])
                        r, b = slice(64 * (j % 2), 64 * (j % 2) + 64), bank_of(key)
                        t = mm(b[:, 0:T], RT[r, 4 + j // 2, i * P:(i + 1) * P], RT[r, 8, :], start=True, stop=True)
                        full(t, key)
                    elif kind == "hx":
                        pe.wait_ge(level_ready, l * 8 + 1)
                        b = bank_of(key)
                        for h in range(N_HG):
                            t = mm(b[:, P * h:P * h + P], E[0][:, h, 0:P], E[0][:, h, P:T], start=True, stop=True)
                        full(t, key)
                    elif kind == "hl":
                        j, hp = s[1], s[2]
                        if j < 8:
                            pe.wait_ge(level_ready, l * 8 + j + 1)
                        b = bank_of(key)
                        for h in range(2):
                            for i in range(NT):
                                hh, lo, c = 2 * hp + h, i * P, P * (2 * h + i)
                                left = (E[j % 2] if j < 8 else kT)[:, hh, lo:lo + P]
                                right = (E[j % 2] if j < 8 else hqT)[:, hh, lo:lo + P]
                                t = mm(b[:, c:c + P], left, right, start=True, stop=True)
                        full(t, key)
                    elif kind == "ho":
                        wait_freed([(l, "hi", 0), (l, "hi", 1), (l, "hx"), (l, "hl", 8, 0), (l, "hl", 8, 1)])
                        b = bank_of(key)
                        for h in range(N_HG):
                            v0, v1 = hv[:, 0, HD * h:HD * h + HD], hv[:, 1, HD * h:HD * h + HD]
                            o0, o1 = b[:, HD * h:HD * h + HD], b[:, T + HD * h:T + HD * h + HD]
                            mm(o0, attT[:, h, 0, :], v0, start=True, stop=True)
                            mm(o1, attX[:, h, :], v0, start=True, stop=False)
                            t = mm(o1, attT[:, h, 1, :], v1, start=False, stop=True)
                        full(t, key)
                    elif kind == "oht":
                        pe.wait_ge(og_ready, l + 1)
                        b = bank_of(key)
                        for i in range(NT):
                            t = turn(b[:, i * P:(i + 1) * P],
                                     og[:, 4 * i + 2 * s[1]:4 * i + 2 * s[1] + 2, :].rearrange("p h d -> p (h d)"),
                                     ident)
                        full(t, key)
                    elif kind in ("dl", "dt", "dp"):
                        attention(dsa[l], kind, s[1])
                wait_freed([(l, "o", pr) for pr in range(3)] + [(l, "pair", pr) for pr in range(3)] +
                           [(l, "oht", f) for f in range(2)])
                for m in range(KD):
                    w = arrived(c0 + 16 + m // 4)[:, :, P * (m % 4):P * (m % 4) + P]
                    b = bank_of((l, "yab", m))
                    for k in range(3):
                        mm(b[:, 0:T], w[:, k, :], osT[:, k, :], start=(k == 0), stop=(k == 2))
                    for k in range(3):
                        t = mm(b[:, T:2 * T], w[:, 3 + k, :], odT[:, k, :], start=(k == 0), stop=(k == 2))
                    full(t, (l, "yab", m))
                    b = bank_of((l, "yh", m))
                    for k in range(2):
                        t = mm(b[:, 0:T], w[:, 6 + k, :], ohT[:, k, :], start=(k == 0), stop=(k == 1))
                    full(t, (l, "yh", m))
                pe.wait_ge(mix_ready, KD * (l + 1))
                for n in range(2):
                    w = arrived(c0 + 18 + n)
                    for i in range(NT):
                        token_major((l, "wo", n, i), w, lambda k: mixT[:, k, :], i)
                turn_rows(2 * l + 1)
                for f in range(NF):
                    w = arrived(c0 + 20 + f // 4)
                    feature_major((l, "up", f), w[:, :, P * (f % 4):P * (f % 4) + P], hT)
                for kb in range(4):
                    for n in range(2):
                        w = arrived(c0 + 28 + 2 * kb + n)
                        for i in range(NT):
                            key = (l, "down", n, i)
                            b = bank_of(key) if kb == 0 else psum[bk.bank(key)]
                            for k in range(KD):
                                pe.wait_ge(hid_ready, NF * l + 8 * kb + k + 1)
                                t = mm(b[:, :], hid[:, 8 * kb + k, i * P:(i + 1) * P], w[:, k, :],
                                       start=(kb == 0 and k == 0), stop=(kb == 3 and k == KD - 1))
                            if kb == 3:
                                full(t, key)
                            elif i == NT - 1:
                                t.then_inc(down_chunk_used, 1)

            c0 = DEPTH * CL
            pe.wait_ge(t5_loaded, 48)
            for g in range(DIL_G):
                b = bank_of((2, "t5", g))
                t = mm(b[0:4, :], t5_tab[:, 4 * g:4 * g + 4], t5_onehot[:, 512 * g:512 * g + 512], start=True, stop=True)
                full(t, (2, "t5", g))
            turn_rows(4)
            w = arrived(c0)
            for i in range(NT):
                token_major((2, "kv", i), w, lambda k: memT[:, k, :], i)
            turn_rows(5)
            for c in range(8):
                w = arrived(c0 + 1 + c)
                for i in range(NT):
                    token_major((2, "p", c, i), w, h_tile, i)
            pe.wait_ge(seg_normed, len(segments))
            for c, (buf, col) in enumerate(tiles2):
                b = bank_of((2, "pt", c))
                for i in range(NT):
                    t = turn(b[:, i * P:(i + 1) * P], buf[:, i, col:col + P], ident)
                full(t, (2, "pt", c))
            wait_freed([(2, "pt", c) for c in range(24)])
            wait_freed([(2, "p", c, i) for c in range(8) for i in range(NT)])
            for kind, u in ATT2_STEPS:
                attention(att2, kind, u)
            wait_freed([(2, "pair", pr) for pr in range(KD)])
            for n in range(2):
                w = arrived(c0 + 9 + n)
                for i in range(NT):
                    token_major((2, "wo", n, i), w, oT2, i)
            turn_rows(6)
            for i in range(NT):
                token_major((2, "router", i), wr, h_tile, i)
            before, ones = sbmask[:, 0:P], sbmask[:, P:2 * P]
            pe.wait_ge(picks_made, 1)
            b, chosen = bank_of((2, "rank")), fine[4]
            mm(b[:, 0:32], before, chosen[:, 0, :], start=True, stop=True)
            mm(b[:, 32:64], ones, chosen[:, 0, :], start=True, stop=False)
            mm(b[:, 32:64], before, chosen[:, 1, :], start=False, stop=True)
            mm(b[:, 64:96], ones, chosen[:, 0, :], start=True, stop=False)
            t = mm(b[:, 64:96], ones, chosen[:, 1, :], start=False, stop=True)
            full(t, (2, "rank"))
            pe.wait_ge(gates_made, 1)
            b = bank_of((2, "gateT"))
            for i in range(NT):
                t = turn(b[0:N_EXP, i * P:(i + 1) * P], fine[2][:, i, :], ident)
            full(t, (2, "gateT"))
            pe.wait_ge(put0_ready, 1)
            rows = put0.rearrange("p i e s -> p i (e s)")
            for j in range(8):
                b = bank_of((2, "put", j))
                for h in range(2):
                    for i in range(NT):
                        t = turn(b[:, T * h + P * i:T * h + P * i + P], rows[:, i, P * (2 * j + h):P * (2 * j + h) + P],
                                 ident)
                full(t, (2, "put", j))
            wait_freed([(2, "put", j) for j in range(8)])
            pe.wait_ge(zeros_set, 1)
            for q in range(4):
                pe.wait_ge(bank_free[4 + q], base[4 + q])
                t = mm(psum[4 + q][:, :], zeros, x[:, 0, 0:512], start=True, stop=False)
            t.then_inc(y_step, 1)
            pe.wait_ge(h_rows_ready, 2)
            picks, puts = pick.rearrange("p i e s -> p i (e s)"), put.rearrange("p e t -> p (e t)")

            def w2_of(q):
                return wslot[q].rearrange("p k n -> p (k n)").rearrange("p (k n) -> p k n", k=4)

            def turn_hidden(e, b):
                rows = slice(64 * e, 64 * e + 64)
                for k in range(4):
                    t = mm(psum[b][:, 64 * k:64 * k + 64], pair_hid[rows, P * k:P * k + P], ident[rows, rows],
                           start=True, stop=True)
                t.then_inc(bank_full[b], 1)

            def expert_out(e, n):
                for k in range(4):
                    t = mm(psum[n][64 * e:64 * e + 64, :], aTs[e][:, k, :],
                           w2_of(3 * e + 2)[:, k, 512 * n:512 * n + 512], start=(k == 0), stop=(k == 3))
                return t

            with pe.Fori(0, ROUNDS) as it:
                for n in range(2):
                    pe.wait_ge(bank_free[n], it * (3 - n) + base[n])
                    for k in range(4):
                        for i in range(NT):
                            t = mm(psum[n][:, P * k:P * k + P], xn3[:, i, 512 * n + P * k:512 * n + P * k + P],
                                   picks[:, i, bass.ds(it * P, P)], start=(i == 0), stop=(i == NT - 1))
                    t.then_inc(bank_full[n], 1)
                pe.wait_ge(bank_free[2], it * 3 + base[2])
                pe.wait_ge(bank_free[3], it * 2 + base[3])
                pe.wait_ge(bank_free[0], it * 3 + (base[0] + 1))
                for e in range(2):
                    for j in range(2):
                        pe.wait_ge(slot_full[3 * e + j], it * 16 + (slot_total[3 * e + j] + 16))
                        for k in range(KD):
                            if (e, j, k) == (0, 0, 4):
                                pe.wait_ge(bank_free[1], it * 2 + (base[1] + 1))
                            t = mm(psum[2 + j][64 * e:64 * e + 64, :], xg[:, k, 64 * e:64 * e + 64],
                                   wslot[3 * e + j][:, k, 0:512], start=(k == 0), stop=(k == KD - 1))
                        t.then_inc(bank_full[2 + j], 1)
                        if (e, j) == (1, 0):
                            pe.wait_ge(bank_free[3], it * 2 + (base[3] + 1))
                            turn_hidden(0, 0)
                pe.wait_ge(slot_full[2], it * 16 + (slot_total[2] + 16))
                pe.wait_ge(bank_free[0], it * 3 + (base[0] + 2))
                expert_out(0, 0)
                pe.wait_ge(bank_free[3], it * 2 + (base[3] + 2))
                turn_hidden(1, 2)
                expert_out(0, 1).then_inc(y_step, 1)
                pe.wait_ge(slot_full[5], it * 16 + (slot_total[5] + 16))
                pe.wait_ge(bank_free[2], it * 3 + (base[2] + 3))
                for n in range(2):
                    expert_out(1, n).then_inc(bank_full[n], 1)
                for k in range(KD):
                    if k == 0:
                        pe.wait_ge(bank_free[0], it * 3 + (base[0] + 3))
                    elif k == 4:
                        pe.wait_ge(bank_free[1], it * 2 + (base[1] + 2))
                    t = mm(psum[4 + k // 2][:, T * (k % 2):T * (k % 2) + T], yslot[:, P * k:P * k + P],
                           puts[:, bass.ds(it * T, T)], start=False, stop=False)
            for q in range(4):
                mm(psum[4 + q][:, :], zeros, x[:, 0, 0:512], start=False, stop=True).then_inc(sums_done, 1)
            for q in range(4):
                pe.wait_ge(bank_free[4 + q], base[4 + q] + 1)
            for q in range(4):
                i, n = q // 2, q % 2
                pe.wait_ge(bank_free[q], base2[q] - 1)
                for k in range(4):
                    t = turn(psum[q][:, P * k:P * k + P], yT[:, 4 * n + k, P * i:P * i + P], ident)
                t.then_inc(bank_full[q], 1)
            pe.wait_ge(overflow_known, 1)
            more = pe.value_load(overflow[0:1, 0:1], min_val=0, max_val=1)
            with pe.If(more > 0):
                for q in range(4):
                    pe.wait_ge(bank_free[q], base2[q])
                for q in range(4):
                    i, n = q // 2, q % 2
                    t = mm(psum[4 + q][:, :], ident, x[:, i, 512 * n:512 * n + 512], start=True, stop=False)
                    if q >= 2:
                        t.then_inc(dense_step, 1)
                with pe.Fori(0, ROUNDS) as it:
                    for e in range(2):
                        for j in range(2):
                            q = 3 * e + j
                            pe.wait_ge(slot_full[q], it * 16 + (slot_total[q] + 16 * ROUNDS + 16))
                        for m in range(4):
                            pe.wait_ge(bank_free[m], it * 2 + (base2[m] + e))
                            for j in range(2):
                                for k in range(KD):
                                    t = mm(psum[m][:, T * j:T * j + T], wslot[3 * e + j][:, k, P * m:P * m + P],
                                           hT[:, k, :], start=(k == 0), stop=(k == KD - 1))
                            t.then_inc(bank_full[m], 1)
                        q = 3 * e + 2
                        pe.wait_ge(slot_full[q], it * 16 + (slot_total[q] + 16 * ROUNDS + 16))
                        w2 = wslot[q].rearrange("p k n -> p (k n)").rearrange("p (k n) -> p k n", k=4)
                        for k in range(4):
                            pe.wait_ge(aT_ready, it * 8 + (4 * e + k + 1))
                            for r in range(4):
                                i, n = r // 2, r % 2
                                t = mm(psum[4 + r][:, :], aT[e][:, k, i * P:(i + 1) * P],
                                       w2[:, k, 512 * n:512 * n + 512], start=False, stop=False)
                        t.then_inc(dense_step, 1)
                for q in range(4):
                    i, n = q // 2, q % 2
                    t = mm(psum[4 + q][:, :], zeros, x[:, i, 512 * n:512 * n + 512], start=False, stop=True)
                t.then_inc(dense_step, 1)

        @block.scalar
        def _(act):
            A_ = nc.scalar.activation
            steps = [0]

            def link(ins):
                ins.then_inc(act_step, 1)
                steps[0] += 1
                act.wait_ge(act_step, steps[0])

            def read(key):
                act.wait_ge(*bk.full(key))
                return psum[bk.bank(key)]

            def free(ins, key):
                ins.then_inc(bank_free[bk.bank(key)], 1)

            def norm(n):
                src, waits, rows, (l, name), gain, dst = norms[n]
                for w in waits:
                    act.wait_ge(*w)
                for i in range(NT):
                    junk = memT_flat[:, D * i:D * i + D] if n == 4 else rows[:, i, :]
                    t = A_(junk, src[:, i, :], ACT.Square, accum_out=ss[:, i:i + 1])
                link(t)
                A_(sd, ss, ACT.Sqrt, bias=eps_c, scale=1.0 / D).then_inc(std_ready, 1)
                act.wait_ge(gain0_loaded, 16)
                if n:
                    act.wait_ge(params_loaded, n_params[0])
                for k in range(0, KD, 2):
                    free(A_(dst[:, k, :], read((l, name, k))[:, 0:T], ACT.Copy, scale=gain[:, k:k + 1]), (l, name, k))

            def attention(at, kind, u):
                segs, i, b0 = at.units[u]
                U = at.first + u
                if kind == "dl":
                    act.wait_ge(rowmax_ready, U + 1)
                    p = at.prb[U % 4][:, 0:T * len(segs)]
                    A_(p, p, ACT.Exp, bias=nmax[:, U % 4:U % 4 + 1], accum_out=esum[:, U % 4:U % 4 + 1]
                       ).then_inc(exps_ready, 1)
                elif kind == "dt":
                    if U >= 3:
                        act.wait_ge(probsT_used, U - 2)
                    for g in range(len(segs)):
                        key = (at.tag, "dt", u, g)
                        src = read(key)[:, 0:T].rearrange("p (s t) -> p s t", s=NT)
                        free(A_(at.prT[U % 3][:, NT * g:NT * g + NT, :], src, ACT.Copy), key)
                elif kind == "dp" and u % 4 == 3:
                    act.wait_ge(probsT_used, U + 1)
                    key = (at.tag, "pair", u // 4)
                    free(A_(at.pair_out(u // 4), psum[bk.bank(key)][:, 0:T], ACT.Copy), key)

            act.wait_ge(eps_set, 1)
            for l in range(DEPTH):
                norm(2 * l)
                if l == 0:
                    act.wait_ge(lb_shifted, 1)
                    A_(lb_e, lb_e, ACT.Exp).then_inc(lb_exps, 1)
                for m in range(3):
                    free(A_(skT[:, m, :], read((l, "sk", m))[:, 0:T], ACT.Copy), (l, "sk", m))
                for i in range(NT):
                    free(A_(sv[:, i, :], read((l, "sv", i))[:, 0:384], ACT.Copy), (l, "sv", i))
                for i in range(NT):
                    b = read((l, "d", i))
                    A_(R[:, i, 0:7, :], b[:, 0:448].rearrange("p (h d) -> p h d", h=7), ACT.Copy)
                    free(A_(dv[:, i, :], b[:, 448:512], ACT.Copy), (l, "d", i))
                for i in range(NT):
                    b = read((l, "iq", i))
                    free(A_(R[:, i, 8:16, :], b[:, :].rearrange("p (h d) -> p h d", h=8), ACT.Copy), (l, "iq", i))
                for i in range(NT):
                    b = read((l, "ik", i))
                    A_(R[:, i, 16, :], b[:, 0:HD], ACT.Copy)
                    A_(R[:, i, 17, :], b[:, 0:HD], ACT.Copy)
                    free(A_(iw[:, i, :], b[:, HD:HD + N_IDX], ACT.Copy, scale=IDX_SCALE), (l, "ik", i))
                act.wait_ge(head_sums, l + 1)
                A_(sd14, ss14, ACT.Sqrt, bias=eps_c, scale=1.0 / HD).then_inc(head_std, 1)
                for m in range(4):
                    if m >= 2:
                        act.wait_ge(*bk.freed((l, "hq", m - 2)))
                    A_(hsg[m % 2], read((l, "hq", m))[:, 0:T], ACT.Sigmoid).then_inc(sig_ready, 1)
                for m in range(4):
                    free(A_(fT[:, m, :], read((l, "hf", m))[:, 0:T], ACT.Sigmoid), (l, "hf", m))
                for i in range(NT):
                    free(A_(hv[:, i, :], read((l, "hi", i))[:, 0:T], ACT.Copy), (l, "hi", i))
                for i in range(NT):
                    act.wait_ge(*bk.freed((l, "hq", 2 + i)))
                    A_(hsg[i], read((l, "hg", i))[:, 0:T], ACT.Sigmoid).then_inc(sig_ready, 1)
                for s in MIX:
                    kind, key = s[0], (l,) + s
                    if kind == "g":
                        free(A_(gT[:, s[1], :], read(key)[:, 0:T], ACT.Copy), key)
                    elif kind == "rt" and s[1] % 2 == 0:
                        free(A_(RT[:, s[1], :], read(key)[:, 0:T], ACT.Copy), key)
                    elif kind == "z":
                        h = s[1]
                        if h >= 2:
                            act.wait_ge(*bk.full((l, "u", h - 2)))
                        L = sbL[h % 2]
                        link(A_(L, read(key)[:, 0:384], ACT.Abs))
                        link(A_(L, L, ACT.Exp, scale=-1.0))
                        A_(L, L, ACT.Ln, bias=1.0).then_inc(log1p_ready, 1)
                    elif kind == "u":
                        act.wait_ge(*bk.freed(key))
                        w_ = sbA[s[1] % 4]
                        A_(w_, w_, ACT.Exp).then_inc(sba_ready, 1)
                    elif kind == "o":
                        free(A_(osT[:, s[1], :], read(key)[:, 0:T], ACT.Copy), key)
                    elif kind == "hp":
                        act.wait_ge(f_ready, l + 1)
                        A_(fT, fT, ACT.Ln).then_inc(logf_ready, 1)
                    elif kind == "ix":
                        n = l * 16 + 8 * s[1] + s[2]
                        if n >= 2:
                            act.wait_ge(rel_used, n - 1)
                        free(A_(rel[n % 2], read(key)[:, 0:T], ACT.Relu), key)
                    elif kind == "lv":
                        act.wait_ge(level_exponents, l * 8 + s[1] + 1)
                        e = E[s[1] % 2]
                        A_(e, e, ACT.Exp).then_inc(level_exps, 1)
                    elif kind == "hx":
                        free(A_(attX, read(key)[:, :].rearrange("p (h t) -> p h t", h=N_HG), ACT.Copy), key)
                    elif kind == "ho":
                        free(A_(og, read(key)[:, :].rearrange("p (h d) -> p h d", h=8), ACT.Copy), key)
                    elif kind == "on":
                        act.wait_ge(o_sums, l + 1)
                        A_(sd8, ss8, ACT.Sqrt, bias=eps_c, scale=1.0 / HD).then_inc(o_std, 1)
                    elif kind == "oht":
                        free(A_(ohT[:, s[1], :], read(key)[:, 0:T], ACT.Copy), key)
                    elif kind in ("dl", "dt", "dp"):
                        attention(dsa[l], kind, s[1])
                for m in range(24):
                    act.wait_ge(*bk.freed((l, "g", m)))
                A_(gT, gT, ACT.Sigmoid).then_inc(gates_ready, 1)
                norm(2 * l + 1)
                for f in range(NF):
                    if NF * l + f >= 4:
                        act.wait_ge(hid_ready, NF * l + f - 3)
                    free(A_(hrl[f % 4], read((l, "up", f))[:, 0:T], ACT.Relu), (l, "up", f))

            norm(4)
            for i in range(NT):
                free(A_(kv[:, i, :], read((2, "kv", i))[:, :], ACT.Copy), (2, "kv", i))
            norm(5)

            def seg_square(j):
                buf, col, nh, g, sc, c = segments[j]
                w = nh * HD
                for i in range(NT):
                    keys = [(2, "kv", i)] if buf is kv else \
                        [(2, "p", cc, i) for cc in range(col // 512, (col + w - 1) // 512 + 1)]
                    for k in keys:
                        act.wait_ge(*bk.freed(k))
                if j >= 1:
                    act.wait_ge(seg_sums, j)
                src = buf[:, :, col:col + w]
                dst = squares[:, 0:NT * w].rearrange("p (i f) -> p i f", i=NT)
                A_(dst, src, ACT.Square).then_inc(seg_squared, 1)

            def seg_sqrt(j):
                nh = segments[j][2]
                act.wait_ge(seg_sums, j + 1)
                A_(seg_sd[:, :, 0:nh], seg_ss[:, :, 0:nh], ACT.Sqrt, bias=eps_c, scale=1.0 / HD).then_inc(seg_std, 1)

            seg_square(0)
            seg_sqrt(0)
            for c in range(8):
                if c % 2 == 0:
                    for i in range(NT):
                        free(A_(PP[:, i, 512 * c:512 * c + 512], read((2, "p", c, i))[:, :], ACT.Copy), (2, "p", c, i))
                for j in range(1, len(segments)):
                    if segments[j][5] == c:
                        seg_square(j)
                        seg_sqrt(j)
            for c in range(0, 24, 2):
                free(A_(PT[:, c, :], read((2, "pt", c))[:, 0:T], ACT.Copy), (2, "pt", c))
            for kind, u in ATT2_STEPS:
                attention(att2, kind, u)
            for n in range(NCH - SLOTS, NCH):
                act.wait_ge(*last_use[n])
            for w in wo_done[2]:
                act.wait_ge(*w)
            for q in (1, 4, 5):
                load_expert(act, q, q // 3)
            norm(6)
            act.wait_ge(router_shifted, 1)
            A_(grp[1], grp[1], ACT.Exp)
            A_(one[4], one[4], ACT.Exp).then_inc(router_exps, 1)
            for j in range(0, 8, 2):
                key = (2, "put", j)
                free(A_(put[:, 2 * j:2 * j + 2, :], read(key)[:, :].rearrange("p (e t) -> p e t", e=2), ACT.Copy), key)

            def expert_round(it, load_next):
                act.wait_ge(bank_full[0], it * 3 + (base[0] + 1))
                A_(xg[:, 0:4, :], psum[0][:, :].rearrange("p (k s) -> p k s", k=4), ACT.Copy).then_inc(bank_free[0], 1)
                for e in range(2):
                    rows, b = slice(64 * e, 64 * e + 64), 2 * e
                    act.wait_ge(bank_full[2], it * 3 + (base[2] + e + 1))
                    A_(pair_hid[rows, :], psum[2][rows, :], ACT.Sigmoid).then_inc(experts_up, 1)
                    if load_next:
                        act.wait_ge(bank_full[3], it * 2 + (base[3] + e + 1))
                        load_expert(act, 3 * e + 1, it * 2 + (2 + e))
                    act.wait_ge(bank_full[b], it * 3 + (base[b] + 2 + e))
                    A_(aTs[e], psum[b][:, 0:256].rearrange("p (k s) -> p k s", k=4), ACT.Copy
                       ).then_inc(bank_free[b], 1)
                act.wait_ge(bank_full[0], it * 3 + (base[0] + 3))
                A_(yslot[:, 0:512], psum[0][:, :], ACT.Copy).then_inc(bank_free[0], 1)
                if load_next:
                    act.wait_ge(bank_full[1], it * 2 + (base[1] + 2))
                    load_expert(act, 5, it * 2 + 3)

            with act.Fori(0, ROUNDS - 1) as it:
                expert_round(it, True)
            expert_round(ROUNDS - 1, False)
            for q in (0, 2):
                act.wait_ge(sums_done, q + 1)
                A_(yT[:, 2 * q:2 * q + 2, :], psum[4 + q][:, :].rearrange("p (k t) -> p k t", k=2), ACT.Copy
                   ).then_inc(bank_free[4 + q], 1)
            act.wait_ge(overflow_known, 1)
            more = act.value_load(overflow[0:1, 0:1], min_val=0, max_val=1)
            with act.If(more > 0):
                with act.Fori(0, ROUNDS) as it:
                    for e in range(2):
                        for m in range(4):
                            if m >= 2:
                                act.wait_ge(bank_free[m - 2], it * 2 + (base2[m - 2] + e + 1))
                            else:
                                act.wait_ge(bank_free[m + 2], it * 2 + (base2[m + 2] + e))
                            act.wait_ge(bank_full[m], it * 2 + (base2[m] + e + 1))
                            A_(sgm[m % 2], psum[m][:, 0:T], ACT.Sigmoid).then_inc(sig2_ready, 1)

        @block.vector
        def _(dve):
            V = nc.vector
            steps = [0]

            def link(ins):
                ins.then_inc(dve_step, 1)
                steps[0] += 1
                dve.wait_ge(dve_step, steps[0])

            def read(key):
                dve.wait_ge(*bk.full(key))
                return psum[bk.bank(key)]

            def free(ins, key):
                ins.then_inc(bank_free[bk.bank(key)], 1)

            def own(key):
                dve.wait_ge(*bk.freed(key))

            def bc(ap, dims):
                return ap.broadcast_to([P] + dims)

            def norm(n):
                src, waits, rows, (l, name), gain, dst = norms[n]
                dve.wait_ge(std_ready, n + 1)
                link(V.reciprocal(rstd, sd))
                for i in range(NT):
                    V.tensor_scalar(rows[:, i, :], src[:, i, :], rstd[:, i:i + 1], None, ALU.mult
                                    ).then_inc(rows_normed, 1)
                dve.wait_ge(gain0_loaded, 16)
                if n:
                    dve.wait_ge(params_loaded, n_params[0])
                for k in range(1, KD, 2):
                    free(V.tensor_scalar(dst[:, k, :], read((l, name, k))[:, 0:T], gain[:, k:k + 1], None, ALU.mult),
                         (l, name, k))

            def attention(at, kind, u):
                segs, i, b0 = at.units[u]
                U, p = at.first + u, at.prb[(at.first + u) % 4]
                if kind == "dl":
                    if u >= 4:
                        for g in range(len(at.units[u - 4][0])):
                            dve.wait_ge(*bk.full((at.tag, "dt", u - 4, g)))
                    if U >= 4:
                        dve.wait_ge(exps_ready, U - 3)
                    for g, (_, _, bias, _) in enumerate(segs):
                        key = (at.tag, "dl", u, g)
                        free(V.tensor_tensor_reduce(out=p[:, T * g:T * g + T], in0=read(key)[:, 0:T], in1=bias,
                                                    scale=1.0, scalar=-3.0e38, op0=ALU.add, op1=ALU.max,
                                                    accum_out=mx[:, U % 4, g:g + 1]), key)
                    for g in range(len(segs)):
                        own((at.tag, "dl", u, g))
                    V.tensor_reduce(nmax[:, U % 4:U % 4 + 1], mx[:, U % 4, 0:len(segs)], AX.X, ALU.max, negate=True
                                    ).then_inc(rowmax_ready, 1)
                elif kind == "dn":
                    dve.wait_ge(exps_ready, U + 1)
                    link(V.reciprocal(rsum[:, U % 4:U % 4 + 1], esum[:, U % 4:U % 4 + 1]))
                    w = T * len(segs)
                    V.tensor_scalar(p[:, 0:w], p[:, 0:w], rsum[:, U % 4:U % 4 + 1], None, ALU.mult
                                    ).then_inc(probs_ready, 1)

            V.memset(eps_c, EPS).then_inc(eps_set, 1)
            dve.wait_ge(consts_loaded, 16)

            def lower_bounds():
                dve.wait_ge(params_loaded, n_params[0])
                link(V.tensor_tensor(lb_m, lbraw[:, 0, :], lbraw[:, 1, :], ALU.max))
                for l in range(DEPTH):
                    t = V.tensor_tensor(lb_e[:, l, :], lbraw[:, l, :], lb_m, ALU.subtract)
                t.then_inc(lb_shifted, 1)
                dve.wait_ge(lb_exps, 1)
                link(V.tensor_tensor(lb_s, lb_e[:, 0, :], lb_e[:, 1, :], ALU.add))
                link(V.reciprocal(lb_r, lb_s))
                for l in range(DEPTH):
                    t = V.tensor_tensor(lb_e[:, l, :], lb_e[:, l, :], lb_r, ALU.mult)
                link(t)
                V.tensor_tensor(lb[:, 0, :], lb_e[:, 0, :], lb_e[:, 0, :], ALU.subtract)
                link(V.tensor_tensor(lb_s, lb_e[:, 0, :], lb_e[:, 1, :], ALU.add))
                link(V.tensor_tensor(lb[:, 1, :], lb_s, lb_e[:, 0, :], ALU.subtract))
                link(V.tensor_scalar(omlb, lb, -1.0, 1.0, ALU.mult, ALU.add))

            for l in range(DEPTH):
                norm(2 * l)
                if l == 0:
                    lower_bounds()
                for m in range(3):
                    free(V.tensor_scalar(sqT[:, m, :], read((l, "sq", m))[:, 0:T], HD ** -0.5, None, ALU.mult),
                         (l, "sq", m))
                for n in ("d", "iq", "ik"):
                    for i in range(NT):
                        dve.wait_ge(*bk.freed((l, n, i)))
                q7 = R[:, :, 0:7, :]
                for i in range(NT):
                    t = V.tensor_tensor(sq14[:, i], R[:, i, 0:7, :], R[:, i, 0:7, :], ALU.mult)
                link(t)
                V.tensor_reduce(ss14, sq14, AX.X, ALU.add).then_inc(head_sums, 1)
                for m in range(4):
                    dve.wait_ge(sig_ready, 6 * l + m + 1)
                    free(V.tensor_tensor(hqT[:, m, :], read((l, "hq", m))[:, 0:T], hsg[m % 2], ALU.mult), (l, "hq", m))
                dve.wait_ge(head_std, l + 1)
                link(V.reciprocal(r14, sd14))
                link(V.tensor_scalar(r14[:, :, 0:N_DSA], r14[:, :, 0:N_DSA], HD ** -0.5, None, ALU.mult))
                for i in range(NT):
                    t = V.tensor_tensor(R[:, i, 0:7, :], R[:, i, 0:7, :], bc(r14[:, i, :].unsqueeze(2), [7, HD]), ALU.mult)
                link(t)
                for i in range(NT):
                    V.tensor_tensor(R[:, i, 0:N_DSA, :], R[:, i, 0:N_DSA, :],
                                    bc(qn[:, l, :].unsqueeze(1), [N_DSA, HD]), ALU.mult)
                    t = V.tensor_tensor(R[:, i, 6, :], R[:, i, 6, :], kn[:, l, :], ALU.mult)
                link(t)
                link(V.tensor_copy(R[:, :, 7, :], R[:, :, 6, :]))
                a1 = ra[:, 0:288].rearrange("p (i h d) -> p i h d", i=NT, h=RH)
                a2 = ra[:, 288:576].rearrange("p (i h d) -> p i h d", i=NT, h=RH)
                a3 = ra[:, 576:864].rearrange("p (i h d) -> p i h d", i=NT, h=RH)
                x1, x2 = R[:, :, :, 0:8], R[:, :, :, 8:16]
                co = bc(cosT.unsqueeze(2), [NT, RH, 8])
                si = bc(sinT.unsqueeze(2), [NT, RH, 8])
                V.tensor_tensor(a1, x1, co, ALU.mult)
                V.tensor_tensor(a2, x2, si, ALU.mult)
                link(V.tensor_tensor(a3, x1, si, ALU.mult))
                link(V.tensor_tensor(x1, a1, a2, ALU.subtract))
                link(V.tensor_tensor(a1, x2, co, ALU.mult))
                V.tensor_tensor(x2, a1, a3, ALU.add).then_inc(R_ready, 1)
                for i in range(NT):
                    dve.wait_ge(sig_ready, 6 * l + 4 + i + 1)
                    free(V.tensor_tensor(hgs[:, i, :], read((l, "hg", i))[:, 0:T], hsg[i], ALU.mult), (l, "hg", i))

                for s in MIX:
                    kind, key = s[0], (l,) + s
                    if kind == "rt" and s[1] % 2 == 1:
                        free(V.tensor_copy(RT[:, s[1], :], read(key)[:, 0:T]), key)
                    elif kind == "z":
                        h, L = s[1], sbL[s[1] % 2]
                        dve.wait_ge(log1p_ready, l * N_SB + h + 1)
                        free(V.scalar_tensor_tensor(out=L, in0=read(key)[:, 0:384], scalar=0.0, in1=L,
                                                    op0=ALU.max, op1=ALU.add), key)
                        own(key)
                        V.tensor_tensor(L, L, sbmask, ALU.mult).then_inc(sp_ready, 1)
                    elif kind == "u":
                        h = s[1]
                        if h >= 4:
                            dve.wait_ge(*bk.full((l, "o", (h - 4) // 2)))
                        free(V.tensor_tensor(sbA[h % 4], read(key)[:, 0:384], sbneg, ALU.add), key)
                    elif kind == "hp":
                        for m in range(N_HG):
                            dve.wait_ge(*bk.freed((l, "hf", m)))
                            t = V.tensor_scalar(fT[:, m, :], fT[:, m, :], omlb[:, l, m:m + 1], lb[:, l, m:m + 1],
                                                ALU.mult, ALU.add)
                        link(t)
                        link(V.tensor_scalar(kT, fT, -1.0, 1.0, ALU.mult, ALU.add))
                        V.tensor_scalar(fT, fT, F_MIN, None, ALU.max).then_inc(f_ready, 1)
                        link(V.memset(attT, 0.0))
                        dve.wait_ge(logf_ready, l + 1)
                        for m in range(N_HG):
                            t = V.tensor_tensor_scan(bT[:, m, :], scan0, fT[:, m, :], 0.0, ALU.mult, ALU.add)
                        link(t)
                    elif kind == "ix":
                        i, j = s[1], s[2]
                        n = l * 16 + 8 * i + j
                        dve.wait_ge(*bk.freed(key))
                        if j == 0:
                            t = V.tensor_scalar(score[:, i, :], rel[n % 2], iw[:, i, 0:1], None, ALU.mult)
                        else:
                            t = V.scalar_tensor_tensor(out=score[:, i, :], in0=rel[n % 2], scalar=iw[:, i, j:j + 1],
                                                       in1=score[:, i, :], op0=ALU.mult, op1=ALU.add)
                        t.then_inc(rel_used, 1)
                        dve.wait_ge(rel_used, n + 1)
                    elif kind == "tk":
                        i = s[1]
                        sc, sel = score[:, i, :], negsel[:, i, :]
                        link(V.tensor_scalar(sel, causal[:, i, :], -1.0, -NEG, ALU.add, ALU.mult))
                        link(V.tensor_tensor(sc, sc, sel, ALU.add))
                        for _ in range(TOPK // 8):
                            link(V.max(out=top8, in_=sc))
                            link(V.match_replace(out=sc, in_to_replace=top8, in_values=sc, imm_value=-3.0e38))
                        link(V.tensor_scalar(sel, sc, -2.0e38, None, ALU.is_le))
                        link(V.tensor_tensor(sel, sel, causal[:, i, :], ALU.mult))
                        link(V.tensor_scalar(sel, sel, -1.0, -NEG, ALU.add, ALU.mult))
                    elif kind == "lv":
                        j, e = s[1], E[s[1] % 2]
                        if j < 2:
                            dve.wait_ge(*bk.full((l, "o", 2)))
                        elif j == 2:
                            dve.wait_ge(*bk.full((l, "hx")))
                        else:
                            dve.wait_ge(*bk.full((l, "hl", j - 2, 1)))
                        if j == 0:
                            b4 = bT.rearrange("p h (n c) -> p h n c", c=HG_CHUNK)
                            e4 = e.rearrange("p h (n c) -> p h n c", c=HG_CHUNK)
                            end = b4[:, :, :, HG_CHUNK - 1:HG_CHUNK]
                            link(V.tensor_tensor(e4[:, :, 0:2, :], bc(end[:, :, 0:2, :], [4, 2, HG_CHUNK]),
                                                 b4[:, :, 0:2, :], ALU.subtract))
                            V.tensor_tensor(e4[:, :, 0, :], e4[:, :, 0, :], bc(end[:, :, 1, :], [4, HG_CHUNK]), ALU.add)
                            V.tensor_copy(e4[:, :, 2, :], b4[:, :, 2, :])
                            t = V.tensor_tensor(e4[:, :, 3, :], b4[:, :, 3, :], bc(end[:, :, 2, :], [4, HG_CHUNK]), ALU.add)
                        else:
                            half = HG_CHUNK >> (j - 1)
                            m = N_HG * T // (2 * half)
                            bv = bT.rearrange("p h t -> p (h t)").rearrange("p (m s c) -> p m s c", s=2, c=half)
                            ev = e.rearrange("p h t -> p (h t)").rearrange("p (m s c) -> p m s c", s=2, c=half)
                            end = bc(bv[:, :, 0, half - 1:half], [m, half])
                            V.tensor_tensor(ev[:, :, 0, :], end, bv[:, :, 0, :], ALU.subtract)
                            if j == 1:
                                t = V.tensor_copy(ev[:, :, 1, :], bv[:, :, 1, :])
                            else:
                                t = V.tensor_tensor(ev[:, :, 1, :], bv[:, :, 1, :], end, ALU.subtract)
                        t.then_inc(level_exponents, 1)
                    elif kind == "lm":
                        j, e = s[1], E[s[1] % 2]
                        half = P if j == 0 else HG_CHUNK >> (j - 1)
                        dve.wait_ge(level_exps, l * 8 + j + 1)
                        ev, kv_, qv_ = [z.rearrange("p h t -> p (h t)").rearrange("p (m s c) -> p m s c", s=2, c=half)
                                        for z in (e, kT, hqT)]
                        V.tensor_tensor(ev[:, :, 0, :], ev[:, :, 0, :], kv_[:, :, 0, :], ALU.mult)
                        V.tensor_tensor(ev[:, :, 1, :], ev[:, :, 1, :], qv_[:, :, 1, :], ALU.mult
                                        ).then_inc(level_ready, 1)
                    elif kind == "hl":
                        j, hp = s[1], s[2]
                        dst = attT[:, 2 * hp:2 * hp + 2, :, :].rearrange("p h i t -> p (h i) t")
                        msk = bc(hgmask[:, j - 1, :].unsqueeze(1), [4, P]).bitcast(U32)
                        if j > 1:
                            own((l, "hl", j - 1, hp))
                        free(V.copy_predicated(dst, msk, read(key)[:, :].rearrange("p (m t) -> p m t", m=4)), key)
                    elif kind == "ho":
                        dve.wait_ge(*bk.freed(key))
                        link(V.tensor_tensor(og2, og, og, ALU.mult))
                        V.tensor_reduce(ss8, og2, AX.X, ALU.add).then_inc(o_sums, 1)
                    elif kind == "on":
                        dve.wait_ge(o_std, l + 1)
                        link(V.reciprocal(r8, sd8))
                        link(V.tensor_tensor(og, og, bc(r8.unsqueeze(2), [8, HD]), ALU.mult))
                        link(V.tensor_tensor(og, og, bc(onorm[:, l, :].unsqueeze(1), [8, HD]), ALU.mult))
                        V.tensor_tensor(og.rearrange("p h d -> p (h d)"), og.rearrange("p h d -> p (h d)"),
                                        hgs.rearrange("p i f -> p (i f)"), ALU.mult).then_inc(og_ready, 1)
                    elif kind in ("dl", "dn"):
                        attention(dsa[l], kind, s[1])
                dve.wait_ge(gates_ready, l + 1)
                for m in range(KD):
                    y = ymul[m % 2]
                    ga = gT.rearrange("p (b m) t -> p b m t", b=3)
                    free(V.tensor_tensor(y[:, 0:512].rearrange("p (b t) -> p b t", b=2),
                                         read((l, "yab", m))[:, :].rearrange("p (b t) -> p b t", b=2),
                                         ga[:, 0:2, m, :], ALU.mult), (l, "yab", m))
                    free(V.tensor_tensor(y[:, 512:768], read((l, "yh", m))[:, 0:T], ga[:, 2, m, :], ALU.mult),
                         (l, "yh", m))
                    own((l, "yab", m))
                    link(V.tensor_tensor(y[:, 0:T], y[:, 0:T], y[:, T:2 * T], ALU.add))
                    own((l, "yh", m))
                    V.tensor_tensor(mixT[:, m, :], y[:, 0:T], y[:, 512:768], ALU.add).then_inc(mix_ready, 1)
                for n in range(2):
                    for i in range(NT):
                        xs = x[:, i, 512 * n:512 * n + 512]
                        free(V.tensor_tensor(xs, read((l, "wo", n, i))[:, :], xs, ALU.add), (l, "wo", n, i))
                norm(2 * l + 1)
                for f in range(NF):
                    dve.wait_ge(*bk.freed((l, "up", f)))
                    V.tensor_tensor(hid[:, f, :], hrl[f % 4], hrl[f % 4], ALU.mult).then_inc(hid_ready, 1)
                for n in range(2):
                    for i in range(NT):
                        xs = x[:, i, 512 * n:512 * n + 512]
                        free(V.tensor_tensor(xs, read((l, "down", n, i))[:, :], xs, ALU.add), (l, "down", n, i))

            dve.wait_ge(t5_loaded, 48)
            for g in range(DIL_G):
                key, cs = (2, "t5", g), slice(512 * g, 512 * g + 512)
                t = V.tensor_tensor(t5_rows[:, cs], read(key)[0:4, :], t5_mask[:, cs], ALU.add)
                free(t, key)
                own(key)
                V.tensor_copy(t5_rows[:, cs], t5_rows[:, cs]).then_inc(t5_masked, 1)
            norm(4)
            norm(5)

            def seg_sum(j):
                buf, col, nh, g, sc, c = segments[j]
                w = nh * HD
                dve.wait_ge(seg_squared, j + 1)
                src = squares[:, 0:NT * w].rearrange("p (i h d) -> p i h d", i=NT, h=nh)
                V.tensor_reduce(seg_ss[:, :, 0:nh], src, AX.X, ALU.add).then_inc(seg_sums, 1)

            def seg_norm(j):
                buf, col, nh, g, sc, c = segments[j]
                dve.wait_ge(seg_std, j + 1)
                link(V.reciprocal(seg_r[:, :, 0:nh], seg_sd[:, :, 0:nh]))
                if sc != 1.0:
                    link(V.tensor_scalar(seg_r[:, :, 0:nh], seg_r[:, :, 0:nh], sc, None, ALU.mult))
                v = buf[:, :, col:col + nh * HD].rearrange("p i (h d) -> p i h d", h=nh)
                for i in range(NT):
                    t = V.tensor_tensor(v[:, i], v[:, i], bc(seg_r[:, i, 0:nh].unsqueeze(2), [nh, HD]), ALU.mult)
                link(t)
                for i in range(NT):
                    t = V.tensor_tensor(v[:, i], v[:, i], bc(qkg[:, g, :].unsqueeze(1), [nh, HD]), ALU.mult)
                t.then_inc(seg_normed, 1)

            seg_sum(0)
            seg_norm(0)
            dve.wait_ge(bias_loaded, BIASES)
            nb = na_bias.rearrange("p h m c -> p (h m) c")
            link(V.tensor_tensor(nb, nb, bc(nawin.unsqueeze(1), [6 * NA_HEADS, GRID]), ALU.add))
            link(V.memset(zero_bias, 0.0))
            for c in range(8):
                if c % 2 == 1:
                    for i in range(NT):
                        free(V.tensor_copy(PP[:, i, 512 * c:512 * c + 512], read((2, "p", c, i))[:, :]), (2, "p", c, i))
                for j in range(1, len(segments)):
                    if segments[j][5] == c:
                        seg_sum(j)
                        seg_norm(j)
            for c in range(1, 24, 2):
                free(V.tensor_copy(PT[:, c, :], read((2, "pt", c))[:, 0:T]), (2, "pt", c))
            for kind, u in ATT2_STEPS:
                attention(att2, kind, u)
            for n in range(2):
                for i in range(NT):
                    xs = x[:, i, 512 * n:512 * n + 512]
                    free(V.tensor_tensor(xs, read((2, "wo", n, i))[:, :], xs, ALU.add), (2, "wo", n, i))
            norm(6)
            dve.wait_ge(gain_row_loaded, 16)
            dve.wait_ge(*bk.full((2, "h2T", KD - 1)))
            for i in range(NT):
                V.tensor_tensor(xn3[:, i, :], xn3[:, i, :], gain_row, ALU.mult).then_inc(h_rows_ready, 1)
            for i in range(NT):
                free(V.tensor_tensor(rl[:, i, :], read((2, "router", i))[:, 0:36], rbias, ALU.add), (2, "router", i))
            own((2, "router", 0))
            own((2, "router", 1))
            gl, fl = rl[:, :, 0:N_GRP], rl[:, :, N_GRP:36]
            gd, fd = bc(desc[:, N_EXP - N_GRP:].unsqueeze(1), [NT, N_GRP]), bc(desc.unsqueeze(1), [NT, N_EXP])

            def top(out_, vals, down, n, mxv, tmp):
                link(V.tensor_reduce(mxv, vals, AX.X, ALU.max))
                link(V.tensor_tensor(tmp, vals, bc(mxv, [NT, n]), ALU.is_equal))
                link(V.tensor_tensor(tmp, tmp, down, ALU.mult))
                link(V.tensor_reduce(one[11], tmp, AX.X, ALU.max))
                link(V.tensor_tensor(out_, tmp, bc(one[11], [NT, n]), ALU.is_equal))

            top(grp[0], gl, gd, N_GRP, one[0], grp[2])
            link(V.tensor_tensor(grp[1], gl, bc(one[0], [NT, N_GRP]), ALU.subtract))
            link(V.tensor_scalar(grp[3], grp[0], -1.0, -NEG, ALU.add, ALU.mult))
            for i in range(NT):
                t = V.tensor_tensor(fine[0][:, i, :].rearrange("p (g e) -> p g e", g=N_GRP),
                                    fl[:, i, :].rearrange("p (g e) -> p g e", g=N_GRP),
                                    bc(grp[3][:, i, :].unsqueeze(2), [N_GRP, EPG]), ALU.add)
            link(t)
            top(fine[1], fine[0], fd, N_EXP, one[1], fine[4])
            link(V.tensor_scalar(fine[2], fine[1], NEG * 10, None, ALU.mult))
            link(V.tensor_tensor(fine[2], fine[2], fine[0], ALU.add))
            top(fine[3], fine[2], fd, N_EXP, one[2], fine[4])
            V.tensor_tensor(one[4], one[2], one[1], ALU.subtract).then_inc(router_shifted, 1)
            V.tensor_tensor(fine[4], fine[1], fine[3], ALU.add).then_inc(picks_made, 1)
            dve.wait_ge(router_exps, 1)
            link(V.tensor_reduce(one[5], grp[1], AX.X, ALU.add))
            link(V.tensor_scalar(one[6], one[4], 1.0, None, ALU.add))
            link(V.tensor_tensor(one[5], one[5], one[6], ALU.mult))
            link(V.reciprocal(one[7], one[5]))
            link(V.tensor_tensor(one[8], one[7], one[4], ALU.mult))
            link(V.tensor_tensor(fine[1], fine[1], bc(one[7], [NT, N_EXP]), ALU.mult))
            link(V.tensor_tensor(fine[3], fine[3], bc(one[8], [NT, N_EXP]), ALU.mult))
            link(V.tensor_tensor(fine[5], fine[1], fine[3], ALU.add))
            rk = read((2, "rank"))
            dve.wait_ge(picks_made, 1)
            link(V.scalar_tensor_tensor(out=fine[0], in0=rk[:, 0:64].rearrange("p (i e) -> p i e", i=NT), scalar=1.0,
                                        in1=fine[4], op0=ALU.add, op1=ALU.mult))
            link(V.tensor_reduce(one[10][0:1, 0, :], rk[0:1, 64:96], AX.X, ALU.max))
            free(V.tensor_scalar(overflow[0:1, 0:1], one[10][0:1, 0, :], float(CAP), None, ALU.is_gt), (2, "rank"))
            own((2, "rank"))
            V.tensor_copy(overflow[0:1, 1:2], overflow[0:1, 0:1]).then_inc(overflow_known, 1)
            link(V.tensor_scalar(fine[0], fine[0], -1.0, None, ALU.add))
            V.scalar_tensor_tensor(out=fine[2], in0=fine[0], scalar=float(CAP), in1=fine[5], op0=ALU.is_ge,
                                   op1=ALU.mult).then_inc(gates_made, 1)
            V.memset(zeros, 0.0).then_inc(zeros_set, 1)
            for i in range(NT):
                t = V.tensor_tensor(pick[:, i], bc(slot_no.unsqueeze(1), [N_EXP, 64]),
                                    bc(fine[0][:, i, :].unsqueeze(2), [N_EXP, 64]), ALU.is_equal)
            t.then_inc(pick_ready, 1)
            dve.wait_ge(pick_ready, 1)
            for i in range(NT):
                t = V.tensor_tensor(put0[:, i], pick[:, i], bc(fine[5][:, i, :].unsqueeze(2), [N_EXP, 64]), ALU.mult)
            t.then_inc(put0_ready, 1)
            t = V.tensor_copy(gateT[0:N_EXP, :], read((2, "gateT"))[0:N_EXP, 0:T])
            free(t, (2, "gateT"))
            own((2, "gateT"))
            V.tensor_copy(gateT[N_EXP:N_EXP + 1, 0:8], gateT[0:1, 0:8]).then_inc(gateT_ready, 1)
            for j in range(1, 8, 2):
                key = (2, "put", j)
                free(V.tensor_copy(put[:, 2 * j:2 * j + 2, :], read(key)[:, :].rearrange("p (e t) -> p e t", e=2)), key)
            with dve.Fori(0, ROUNDS) as it:
                dve.wait_ge(bank_full[1], it * 2 + (base[1] + 1))
                V.tensor_copy(xg[:, 4:8, :], psum[1][:, :].rearrange("p (k s) -> p k s", k=4)).then_inc(bank_free[1], 1)
                for e in range(2):
                    rows = slice(64 * e, 64 * e + 64)
                    dve.wait_ge(experts_up, it * 2 + (e + 1))
                    V.tensor_tensor(hms[rows, :], psum[2][rows, :], pair_hid[rows, :], ALU.mult).then_inc(bank_free[2], 1)
                    dve.wait_ge(bank_free[2], it * 3 + (base[2] + e + 1))
                    dve.wait_ge(bank_full[3], it * 2 + (base[3] + e + 1))
                    V.tensor_tensor(pair_hid[rows, :], psum[3][rows, :], hms[rows, :], ALU.mult).then_inc(bank_free[3], 1)
                dve.wait_ge(bank_full[1], it * 2 + (base[1] + 2))
                V.tensor_copy(yslot[:, 512:1024], psum[1][:, :]).then_inc(bank_free[1], 1)
            for q in (1, 3):
                dve.wait_ge(sums_done, q + 1)
                V.tensor_copy(yT[:, 2 * q:2 * q + 2, :], psum[4 + q][:, :].rearrange("p (k t) -> p k t", k=2)
                              ).then_inc(bank_free[4 + q], 1)
            for q in range(4):
                i, n = q // 2, q % 2
                dve.wait_ge(bank_full[q], base2[q])
                xs = x[:, i, 512 * n:512 * n + 512]
                V.tensor_tensor(xs, psum[q][:, :], xs, ALU.add).then_inc(bank_free[q], 1)
            dve.wait_ge(overflow_known, 1)
            more = dve.value_load(overflow[0:1, 0:1], min_val=0, max_val=1)
            with dve.If(more > 0):
                with dve.Fori(0, ROUNDS) as it:
                    for e in range(2):
                        dve.wait_ge(gate_row[e], it * 16 + 16)
                        dve.wait_ge(dense_step, it * 2 + (e + 1))
                        for m in range(4):
                            g = 4 * e + m
                            a_, b_ = psum[m][:, 0:T], psum[m][:, T:2 * T]
                            dve.wait_ge(sig2_ready, it * 8 + (g + 1))
                            V.tensor_tensor(hm[2 * (m % 2)], a_, sgm[m % 2], ALU.mult).then_inc(dve_step, 1)
                            dve.wait_ge(dve_step, it * 8 + (steps[0] + g + 1))
                            V.tensor_tensor(hm[2 * (m % 2) + 1], b_, hm[2 * (m % 2)], ALU.mult
                                            ).then_inc(bank_free[m], 1)
                            dve.wait_ge(bank_free[m], it * 2 + (base2[m] + e + 1))
                            V.tensor_tensor(aT[e][:, m, :], hm[2 * (m % 2) + 1], gate[e], ALU.mult
                                            ).then_inc(aT_ready, 1)
                dve.wait_ge(dense_step, N_EXP + 3)
                for q in range(4):
                    i, n = q // 2, q % 2
                    V.tensor_copy(x[:, i, 512 * n:512 * n + 512], psum[4 + q][:, :])
            V.memset(one[0], 0.0).then_inc(out_ready, 1)


def host_constants():
    p, j = np.arange(P)[:, None], np.arange(P)[None, :]
    f = np.float32
    past = (p < j).astype(f)
    cols = [np.eye(P, dtype=f), -(p >= j).astype(f), -np.ones((P, P), f)]
    sbmask = np.concatenate([past, np.ones((P, P), f), past], axis=1)
    cols += [sbmask, (sbmask - 1) * f(1e30)]
    t = np.arange(T)[None, :]
    cols += [(t <= p + P * i).astype(f) for i in range(NT)]
    for lev in range(1, 8):
        h = HG_CHUNK >> (lev - 1)
        cols.append(((p // (2 * h) == j // (2 * h)) & (p % (2 * h) < h) & (j % (2 * h) >= h)).astype(f))
    cols.append(np.eye(P, dtype=f))
    cols.append(np.broadcast_to((t % HG_CHUNK != 0).astype(f), (P, T)))
    inv = f(500000.0) ** (-(np.arange(8, dtype=f) * f(2.0)) / f(16))
    ang = np.arange(T, dtype=f)[:, None] * inv[None, :].astype(f)
    for fn in (np.cos, np.sin):
        cols += [fn(ang[i * P:(i + 1) * P]).astype(f) for i in range(NT)]
    c, k = (np.arange(P) % GRID)[:, None], np.arange(GRID)[None, :]
    c0 = np.clip(c - 8, 0, GRID - 16)
    cols.append(np.where((k >= c0) & (k < c0 + 16), 0, NEG).astype(f))
    cols.append(np.broadcast_to((N_EXP - np.arange(N_EXP)).astype(f), (P, N_EXP)))
    s = np.arange(64)
    cols.append(np.broadcast_to(np.where(s < CAP, s, -5).astype(f), (P, 64)))
    main = np.ascontiguousarray(np.concatenate(cols, axis=1))
    delta = np.arange(512) - (T - 1)
    n = np.abs(delta)
    large = 8 + (np.log(np.maximum(n, 1).astype(f) / f(8)) / f(math.log(1024 / 8)) * f(8)).astype(np.int32)
    bucket = (delta > 0) * 16 + np.where(n < 8, n, np.minimum(large, 15))
    onehot, mask = np.zeros((32, 3, 512), f), np.zeros((4, 3, 512), f)
    for g, (win, dil) in enumerate(DIL):
        ok = (delta % dil == 0) & (n <= win // 2)
        onehot[bucket[ok], g, np.nonzero(ok)[0]] = 1
        mask[:, g, ~ok] = NEG
    return {"c_main": main, "c_t5": onehot.reshape(32, -1), "c_t5m": mask.reshape(4, -1)}


_INS = ['x', 'norm_mix', 'w_in', 'qn_dsa', 'kn_dsa', 'hgrn_lb', 'hgrn_onorm', 'w_br_sb', 'w_br_dsa', 'w_br_hgrn',
        'w_out', 'norm_mlp', 'w_up', 'w_down', 'mem_2', 'g_mix_2', 'w_in_2', 'qk_gain_2', 'na_rpb_2', 't5_table_2',
        'g_mem_2', 'w_mem_kv_2', 'w_out_2', 'g_ffn_2', 'w_r1_2', 'b_r1_2', 'w_r2_2', 'b_r2_2', 'w1_2', 'w3_2', 'w2_2']


def kernel(**inputs):
    import concourse.bacc as bacc
    from concourse.bass_utils import run_bass_kernel_spmd

    nc = bacc.Bacc("TRN2", target_bir_lowering=False, num_devices=1)
    arrays, aps = {}, {}
    for name, value in list((n, inputs[n]) for n in _INS) + list(host_constants().items()):
        arrays[f"in_{name}"] = np.ascontiguousarray(value)
        aps[name] = nc.dram_tensor(f"in_{name}", value.shape, F32, kind="ExternalInput").ap()
    out = nc.dram_tensor("out_0", [1, T, D], F32, kind="ExternalOutput").ap()
    build(nc, aps, out)
    result = run_bass_kernel_spmd(nc, [arrays], core_ids=[0])
    return result.results[0]["out_0"]
```
